# Optimizing a Trainium2 kernel written in Bass

```python
import math
import jax, jax.numpy as jnp
from jax import lax
import numpy as np

D_MODEL = 1024
BATCH = 1
SEQ = 2048
DEPTH = 1

CHUNK = 64
Q_BLOCK = 128

HEAD_DIM = 64
D_MIX = D_MODEL

A_HEADS = 8
A_WIDTH = A_HEADS * HEAD_DIM
A_KV_DIM = HEAD_DIM
IDX_HEADS = 4
IDX_DIM = 64
TOPK_MAX = 256

B_HEADS = 8
B_KV_HEADS = 2
B_GROUP = B_HEADS // B_KV_HEADS
B_WIDTH = B_HEADS * HEAD_DIM
WINDOW = 128
WIN_CHUNKS = WINDOW // CHUNK

N_ALIBI = A_HEADS + B_HEADS
ALPHA = (2 * DEPTH) ** 0.25
BETA = (8 * DEPTH) ** -0.25
LN_EPS = 1e-5

SPLITS = (A_WIDTH, A_KV_DIM, A_KV_DIM, A_WIDTH, IDX_HEADS * IDX_DIM, IDX_DIM, IDX_HEADS,
          B_WIDTH, B_KV_HEADS * HEAD_DIM, B_KV_HEADS * HEAD_DIM, B_WIDTH)
IN_COLS = sum(SPLITS)
V_SLICES = (2, 9)

kernel_name = "hybrid_dsa_swa_sink_deepnorm"

def alibi_slopes(n):
    return np.array([2.0 ** (-8.0 * (i + 1) / n) for i in range(n)], dtype=np.float32)

def layer_norm(x, g, b):
    xf = x.astype(jnp.float32)
    mu = jnp.mean(xf, axis=-1, keepdims=True)
    var = jnp.mean(jnp.square(xf - mu), axis=-1, keepdims=True)
    y = (xf - mu) * lax.rsqrt(var + LN_EPS)
    return (y * g.astype(jnp.float32) + b.astype(jnp.float32)).astype(x.dtype)

def sparse_indexed_attention(qa, ka, va, qi, ki, wi, slopes):
    bn, L, _ = qa.shape
    k_top = min(TOPK_MAX, L // 4)
    n_blk = L // Q_BLOCK
    q_b = qa.reshape(bn, n_blk, Q_BLOCK, A_HEADS, HEAD_DIM).transpose(1, 0, 2, 3, 4)
    qi_b = qi.reshape(bn, n_blk, Q_BLOCK, IDX_HEADS, IDX_DIM).transpose(1, 0, 2, 3, 4)
    w_b = wi.reshape(bn, n_blk, Q_BLOCK, IDX_HEADS).transpose(1, 0, 2, 3)
    key_chunk = jnp.arange(L) // CHUNK
    idx_scale = IDX_HEADS ** -0.5 * IDX_DIM ** -0.5
    attn_scale = HEAD_DIM ** -0.5
    slopes = jnp.asarray(slopes)

    def one_block(args):
        blk, q_blk, qi_blk, w_blk = args
        t = blk * Q_BLOCK + jnp.arange(Q_BLOCK)
        t_chunk = t // CHUNK
        dots = jnp.einsum('bqhd,bsd->bqhs', qi_blk, ki).astype(jnp.float32)
        score = jnp.einsum('bqh,bqhs->bqs', w_blk.astype(jnp.float32) * idx_scale,
                           jax.nn.relu(dots))
        visible = key_chunk[None, :] <= t_chunk[:, None]
        score = jnp.where(visible[None], score, -jnp.inf)
        _, idx = lax.top_k(score, k_top)
        k_sel = jax.vmap(lambda kk, ii: kk[ii])(ka, idx)
        v_sel = jax.vmap(lambda vv, ii: vv[ii])(va, idx)
        logits = jnp.einsum('bqhd,bqkd->bqhk', q_blk, k_sel).astype(jnp.float32) * attn_scale
        dist = jnp.abs(t[None, :, None] - idx).astype(jnp.float32)
        logits = logits - slopes[None, None, :, None] * dist[:, :, None, :]
        valid = (idx // CHUNK) <= t_chunk[None, :, None]
        logits = jnp.where(valid[:, :, None, :], logits, -jnp.inf)
        p = jax.nn.softmax(logits, axis=-1).astype(v_sel.dtype)
        return jnp.einsum('bqhk,bqkd->bqhd', p, v_sel)

    out = lax.map(one_block, (jnp.arange(n_blk), q_b, qi_b, w_b))
    return out.transpose(1, 0, 2, 3, 4).reshape(bn, L, A_WIDTH)

def sink_window_attention(qb, kb, vb, sinks, slopes):
    bn, L, _ = qb.shape
    nc = L // CHUNK
    q = qb.reshape(bn, nc, CHUNK, B_KV_HEADS, B_GROUP, HEAD_DIM)
    k = kb.reshape(bn, nc, CHUNK, B_KV_HEADS, HEAD_DIM)
    v = vb.reshape(bn, nc, CHUNK, B_KV_HEADS, HEAD_DIM)
    pad = ((0, 0), (WIN_CHUNKS - 1, 0), (0, 0), (0, 0), (0, 0))
    kp = jnp.pad(k, pad)
    vp = jnp.pad(v, pad)
    k_band = jnp.concatenate([kp[:, j:j + nc] for j in range(WIN_CHUNKS)], axis=2)
    v_band = jnp.concatenate([vp[:, j:j + nc] for j in range(WIN_CHUNKS)], axis=2)
    logits = jnp.einsum('bcqkgd,bcskd->bckgqs', q, k_band).astype(jnp.float32) * HEAD_DIM ** -0.5
    chunk_ids = jnp.arange(nc)[:, None]
    q_pos = chunk_ids * CHUNK + jnp.arange(CHUNK)[None, :]
    k_pos = (chunk_ids - (WIN_CHUNKS - 1)) * CHUNK + jnp.arange(WINDOW)[None, :]
    dist = jnp.abs(q_pos[:, :, None] - k_pos[:, None, :]).astype(jnp.float32)
    sl = jnp.asarray(slopes).reshape(B_KV_HEADS, B_GROUP)
    logits = logits - sl[None, None, :, :, None, None] * dist[None, :, None, None, :, :]
    valid = k_pos >= 0
    logits = jnp.where(valid[None, :, None, None, None, :], logits, -jnp.inf)
    sink = jnp.broadcast_to(sinks.astype(jnp.float32).reshape(1, 1, B_KV_HEADS, B_GROUP, 1, 1),
                            logits.shape[:-1] + (1,))
    p = jax.nn.softmax(jnp.concatenate([logits, sink], axis=-1), axis=-1)[..., :-1]
    out = jnp.einsum('bckgqs,bcskd->bcqkgd', p.astype(v_band.dtype), v_band)
    return out.reshape(bn, L, B_WIDTH)

def hybrid_mixer(x, w_in, w_out, sinks):
    proj = jnp.einsum('bld,dc->blc', x, w_in)
    offsets = [int(o) for o in np.cumsum(SPLITS)[:-1]]
    qa, ka, va, ga, qi, ki, wi, qb, kb, vb, gb = jnp.split(proj, offsets, axis=-1)
    slopes = alibi_slopes(N_ALIBI)
    ya = sparse_indexed_attention(qa, ka, va, qi, ki, wi, slopes[0::2])
    yb = sink_window_attention(qb, kb, vb, sinks, slopes[1::2])
    y = jnp.concatenate([ya * jax.nn.silu(ga), yb * jax.nn.silu(gb)], axis=-1)
    return jnp.einsum('blc,cd->bld', y, w_out)

def setup_inputs(seed: int = 0) -> dict:
    key = jax.random.key(seed)
    k_x, k_in, k_out, k_sink, k_g, k_b = jax.random.split(key, 6)
    x = jax.random.normal(k_x, (BATCH, SEQ, D_MODEL), jnp.float32)
    col_scale = np.concatenate([np.full((s,), BETA if i in V_SLICES else 1.0, np.float32)
                                for i, s in enumerate(SPLITS)])
    w_in = (jax.random.normal(k_in, (DEPTH, D_MODEL, IN_COLS), jnp.float32)
            * (D_MODEL ** -0.5) * jnp.asarray(col_scale))
    w_out = jax.random.normal(k_out, (DEPTH, D_MIX, D_MODEL), jnp.float32) * (D_MIX ** -0.5) * BETA
    sinks = jax.random.normal(k_sink, (DEPTH, B_HEADS), jnp.float32) * 0.5
    ln_g = 1.0 + 0.02 * jax.random.normal(k_g, (DEPTH, D_MODEL), jnp.float32)
    ln_b = 0.02 * jax.random.normal(k_b, (DEPTH, D_MODEL), jnp.float32)
    return {"x": x, "w_in": w_in, "w_out": w_out, "sinks": sinks, "ln_g": ln_g, "ln_b": ln_b}

def reference(x, w_in, w_out, sinks, ln_g, ln_b):
    for layer in range(DEPTH):
        y = hybrid_mixer(x, w_in[layer], w_out[layer], sinks[layer])
        x = layer_norm(ALPHA * x + y, ln_g[layer], ln_b[layer])
    return x


_drawn_inputs = setup_inputs


def setup_inputs(seed=0):
    import zlib

    import numpy as np

    out = dict(_drawn_inputs(seed))
    spreads = {}
    factors = {}
    for name, (base, spread) in spreads.items():
        noise = np.random.default_rng([zlib.crc32(name.encode()), seed]).standard_normal(out[name].shape)
        drawn = base * np.exp(spread * noise) if base else spread * noise
        out[name] = __import__('jax').numpy.asarray(drawn.astype(out[name].dtype))
    for name, factor in factors.items():
        out[name] = (out[name] * factor).astype(out[name].dtype)
    return out
```

```python
from contextlib import ExitStack

import numpy as np

import concourse.bass as bass
from concourse import mybir

F32 = mybir.dt.float32
F32R = mybir.dt.float32r
BF16 = mybir.dt.bfloat16
I32 = mybir.dt.int32
U16 = mybir.dt.uint16
ALU = mybir.AluOpType
ACT = mybir.ActivationFunctionType
AX_X = mybir.AxisListType.X

P = 128
L = 2048
D = 1024
KT = D // P
NB = L // P
NPAIR = NB // 2
HALF = L // 2
H = 8
HD = 64
IH = 4
TOPK = 256
BIG = float(2.0 ** 100)
N_TILES = 20
KEY_TILES = 4
SEG = 4
VN = 196
WIN = 192
ROW_QI, ROW_KI, ROW_KA, ROW_KB, ROW_QA, ROW_QB, ROW_G = 0, 256, 320, 384, 512, 1024, 1536
ALPHA = 2.0 ** 0.25
EPS = 1e-5

def late_segments(half):
    return [(4, 4, False), (8, 4, False), (12, 4, True), (16, 4, True)]

def hybrid_kernel(nc, xT, w_tiles, w_norm, w_out, x_res, sinks, ln_g, ln_b, c_step, c_ident,
                  c_upper, c_rhi, c_rlo, c_extm, c_extk, c_bias, c_sel, proj, masks, y_t, out):
    with ExitStack() as ctx:
        def sem(name):
            return ctx.enter_context(nc.semaphore(name))

        def sb(stack, name, shape, dt):
            return stack.enter_context(nc.sbuf_tensor(name, shape, dt))

        psum = ctx.enter_context(nc.psum_tensor("psum", [P, 8, 512], F32))

        vw = sb(ctx, "vw", [P, NB, 200], F32)
        ident = sb(ctx, "ident", [P, P], F32)
        with ExitStack() as early:
            x_hi = sb(early, "x_hi", [P, KT, HALF], F32R)
            x_lo = sb(early, "x_lo", [P, KT, HALF], F32R)
            raw = sb(early, "raw", [P, 2, KT * P], F32)
            w_hi = sb(early, "w_hi", [P, 2, KT, P], F32R)
            w_lo = sb(early, "w_lo", [P, 2, KT, P], F32R)
            wn_hi = sb(early, "wn_hi", [P, KT, VN], F32R)
            wn_lo = sb(early, "wn_lo", [P, KT, VN], F32R)
            staged = sb(early, "staged", [P, 2, HALF], F32)
            ki_raw = sb(early, "ki_raw", [P, HALF], F32)
            ki_hi = sb(early, "ki_hi", [P, L], F32R)
            ki_lo = sb(early, "ki_lo", [HD, L], F32R)
            qi_raw = sb(early, "qi_raw", [P, IH, 2 * P], F32)
            qi_split = sb(early, "qi_split", [P, IH, 2 * P], F32R)
            relu = sb(early, "relu", [P, IH, 512], F32)
            score = sb(early, "score", [P, 2, L], F32)
            dist = sb(early, "dist", [P, 2, L], F32)
            above = sb(early, "above", [P, 2, L], BF16)
            equal = sb(early, "equal", [P, 2, L], BF16)
            steps = sb(early, "steps", [P, 32], F32)
            trial = sb(early, "trial", [P, 2, 2], F32)
            count = sb(early, "count", [P, 2], F32)
            accept = sb(early, "accept", [P, 2], F32)
            n_above = sb(early, "n_above", [P, 2], F32)
        with ExitStack() as late:
            ka_raw = sb(late, "ka_raw", [P, L], F32)
            ext_raw = sb(late, "ext_raw", [P, L], F32)
            ka_ext = sb(late, "ka_ext", [P, 2, L], F32R)
            ka_mix = sb(late, "ka_mix", [P, L], F32R)
            qa_raw = sb(late, "qa_raw", [P, 2, H, P], F32)
            qb_raw = sb(late, "qb_raw", [P, 2, H, P], F32)
            kb_raw = sb(late, "kb_raw", [P, 2, 2, WIN], F32)
            gate = sb(late, "gate", [P, 2, H, P], F32)
            mask = sb(late, "mask", [P, 2, L], BF16)
            qa_ext = sb(late, "qa_ext", [P, 2, H, P], F32R)
            qa_mix = sb(late, "qa_mix", [P, 2, H, P], F32R)
            qb_mix = sb(late, "qb_mix", [P, 2, H, P], F32R)
            kb_hi = sb(late, "kb_hi", [P, 2, 2, WIN], F32R)
            kb_lo = sb(late, "kb_lo", [HD, 2, 2, WIN], F32R)
            upper = sb(late, "upper", [P, P], F32R)
            r_hi = sb(late, "r_hi", [P, H, P], F32R)
            r_lo = sb(late, "r_lo", [P, H, P], F32R)
            ident4 = sb(late, "ident4", [P, 4, P], BF16)
            sel = sb(late, "sel", [H, H, P], F32)
            bias = sb(late, "bias", [P, H, WIN], F32)
            lb = sb(late, "lb", [P, H, WIN], F32)
            ptb_own = sb(late, "ptb_own", [P, H, P], F32)
            ptb_prev = sb(late, "ptb_prev", [P, H, P], F32)
            prob = sb(late, "prob", [P, 3, 512], F32)
            out_a = sb(late, "out_a", [65, 2, 512], F32)
            y_a = sb(late, "y_a", [P, H, HD], F32)
            y_b = sb(late, "y_b", [P, H, HD], F32)
            yt_sb = sb(late, "yt_sb", [P, 2, H, P], F32)
            junk = sb(late, "junk", [P, 2, 1024], BF16)
            part_max = sb(late, "part_max", [P, 2, H], F32)
            neg_max = sb(late, "neg_max", [P, H], F32)
            sink8 = sb(late, "sink8", [P, H], F32)
            sink1 = sb(late, "sink1", [P, H], F32)
            mb = sb(late, "mb", [P, H], F32)
            mb2 = sb(late, "mb2", [P, H], F32)
            nmb = sb(late, "nmb", [P, H], F32)
            zb = sb(late, "zb", [P, H], F32)
            ez = sb(late, "ez", [P, H], F32)
            sum_b = sb(late, "sum_b", [P, H], F32)
            den_b = sb(late, "den_b", [P, H], F32)
            rec_b = sb(late, "rec_b", [P, H], F32)
            rec_a = sb(late, "rec_a", [P, H], F32)
        with ExitStack() as last:
            wo_raw = sb(last, "wo_raw", [P, KT, D], F32)
            wo_hi = sb(last, "wo_hi", [P, KT, D], F32R)
            wo_lo = sb(last, "wo_lo", [P, KT, D], F32R)
            yt_raw = sb(last, "yt_raw", [P, 2, KT, P], F32)
            yt_hi = sb(last, "yt_hi", [P, 2, KT, P], F32R)
            yt_lo = sb(last, "yt_lo", [P, 2, KT, P], F32R)
            x_row = sb(last, "x_row", [P, 2, D], F32)
            z = sb(last, "z", [P, 2, D], F32)
            gains = sb(last, "gains", [P, D], F32)
            shifts = sb(last, "shifts", [P, D], F32)
            stats = sb(last, "stats", [P, 2, 6], F32)
            moments = sb(last, "moments", [P, 2], F32)
            var_eps = sb(last, "var_eps", [P, 1], F32)
            minus_half = sb(last, "minus_half", [P, 1], F32)
            rstd = sb(last, "rstd", [P, 1], F32)

        raw_in = [sem(f"raw_in{i}") for i in range(2)]
        hi_done = sem("hi_done")
        lo_done = sem("lo_done")
        tile_mm = sem("tile_mm")
        tile_out = sem("tile_out")
        stored = [sem(f"stored{i}") for i in range(2)]
        norm_mm = sem("norm_mm")
        norm_out = sem("norm_out")
        const_in = sem("const_in")
        ki_in = sem("ki_in")
        ki_hi_ok = sem("ki_hi_ok")
        ki_lo_ok = sem("ki_lo_ok")
        qi_in = sem("qi_in")
        qi_hi_ok = sem("qi_hi_ok")
        qi_lo_ok = sem("qi_lo_ok")
        dots = sem("dots")
        relued = sem("relued")
        summed = sem("summed")
        trial_ok = sem("trial_ok")
        counted = sem("counted")
        accepted = sem("accepted")
        prep = sem("prep")
        mask_ok = sem("mask_ok")
        mask_out = sem("mask_out")
        late_in = sem("late_in")
        setup_act = sem("setup_act")
        setup_pool = sem("setup_pool")
        setup_dve = sem("setup_dve")
        block_in = [sem(f"block_in{i}") for i in range(2)]
        rounded = sem("rounded")
        split = sem("split")
        b_logits = sem("b_logits")
        b_biased = sem("b_biased")
        b_step = sem("b_step")
        b_max = sem("b_max")
        b_exp = sem("b_exp")
        b_turned = sem("b_turned")
        b_pt = sem("b_pt")
        b_ptp = sem("b_ptp")
        b_mixed = sem("b_mixed")
        b_y = sem("b_y")
        a_scan = sem("a_scan")
        a_scanned = sem("a_scanned")
        a_neg = sem("a_neg")
        a_negt = sem("a_negt")
        a_ext = sem("a_ext")
        a_logits = sem("a_logits")
        a_prob = sem("a_prob")
        a_used = sem("a_used")
        a_outsb = sem("a_outsb")
        a_turned = sem("a_turned")
        a_rec = sem("a_rec")
        a_y = sem("a_y")
        y_turned = sem("y_turned")
        y_gated = sem("y_gated")
        y_stored = [sem(f"y_stored{i}") for i in range(2)]
        pos_ok = sem("pos_ok")
        wo_in = sem("wo_in")
        wo_split = sem("wo_split")
        row_in = [sem(f"row_in{i}") for i in range(2)]
        yt_hi_ok = sem("yt_hi_ok")
        yt_lo_ok = sem("yt_lo_ok")
        o_mm = sem("o_mm")
        o_z = sem("o_z")
        o_step = sem("o_step")
        o_var = sem("o_var")
        o_rstd = sem("o_rstd")
        o_norm = sem("o_norm")
        o_done = sem("o_done")
        out_dma = [sem(f"out_dma{i}") for i in range(2)]
        fin_dma = sem("fin_dma")

        FIRST_TILE = [KT + 2, KT + 2 + N_TILES + KT]

        def item_of(half, tile):
            return FIRST_TILE[half] + tile

        def segments(half):
            return late_segments(half)

        def units_to(b):
            return (b + 1) * (b + 2)

        def loaded(b):
            return 16 * sum(8 if i >= 2 else 7 for i in range(b % 2, b + 1, 2))

        def nd(p):
            return 2 * P * (p + 1)

        def chunks(p):
            return [(c, min(512, nd(p) - c)) for c in range(0, nd(p), 512)]

        def chunks_before(p):
            return sum(2 * len(chunks(i)) for i in range(1, p))

        PAIRS_AT = {(0, 0): [1], (0, 1): [2], (0, 3): [3],
                    (1, 0): [4], (1, 1): [5], (1, 2): [6], (1, 3): [7]}

        def tile_pairs(engine, g0, n, body):
            if g0 == 0:
                for i in range(n // 2):
                    body(i)
            else:
                with engine.Fori(0, n // 2) as i:
                    body(i)

        def wait_if(engine, s, value):
            if not (isinstance(value, int) and value <= 0):
                engine.wait_ge(s, value)

        def proj_tile(tile, half):
            return proj.rearrange("(t p) n -> t p n", p=P)[bass.ds(tile, 1), :, half * HALF:(half + 1) * HALF] \
                .rearrange("a p n -> p (a n)")

        x_view = xT.rearrange("(k p) t -> k p t", p=P)
        block = ctx.enter_context(nc.Block())

        @block.sync
        def _(sp):
            sp.dma_start(ident[:, :], c_ident).then_inc(const_in, 16)
            sp.dma_start(steps[:, :], c_step).then_inc(const_in, 16)

            def load_tiles(half, first, n):
                base = item_of(half, first)

                def body(i):
                    for u in range(2):
                        sp.wait_ge(lo_done, i * 2 + (base + u - 1))
                        sp.dma_start(raw[:, u, :], w_tiles[bass.ds(i * 2 + (first + u), 1), :, :]
                                     .rearrange("a p n -> p (a n)")).then_inc(raw_in[u], 16)

                tile_pairs(sp, half * N_TILES + first, n, body)

            for half in range(2):
                base = item_of(half, 0) - KT - (2 if half == 0 else 0)
                for k in range(KT):
                    n = base + k
                    if n >= 2:
                        sp.wait_ge(lo_done, n - 1)
                    sp.dma_start(raw[:, n % 2, :], x_view[k, :, half * HALF:(half + 1) * HALF]) \
                        .then_inc(raw_in[n % 2], 16)
                if half == 0:
                    for j in range(2):
                        n = KT + j
                        sp.wait_ge(lo_done, n - 1)
                        sp.dma_start(raw[:, n % 2, 0:4 * VN],
                                     w_norm[:, 4 * j:4 * j + 4, :].rearrange("p k n -> p (k n)")) \
                            .then_inc(raw_in[n % 2], 16)
                load_tiles(half, 0, KEY_TILES)
                for i in range(2):
                    sp.wait_ge(stored[i], 16 * (half * N_TILES // 2 + 2))
                if half == 1:
                    sp.wait_ge(ki_lo_ok, 1)
                for r in range(2):
                    sp.dma_start(ki_raw[HD * r:HD * r + HD, :],
                                 proj[ROW_KI:ROW_KI + HD, half * HALF:(half + 1) * HALF]) \
                        .then_inc(ki_in, 16)
                for g, (first, n, _) in enumerate(segments(half)):
                    for p in PAIRS_AT.get((half, g), []):
                        if p > 1:
                            sp.wait_ge(qi_lo_ok, p - 1)
                        for r in range(2):
                            sp.dma_start(qi_raw[HD * r:HD * r + HD, :, :],
                                         proj[ROW_QI:ROW_QI + IH * HD, 2 * P * p:2 * P * p + 2 * P]
                                         .rearrange("(h d) t -> d h t", d=HD)).then_inc(qi_in, 16)
                    load_tiles(half, first, n)

            for i in range(2):
                sp.wait_ge(stored[i], 16 * N_TILES)
            sp.wait_ge(mask_out, 16 * 2 * (NPAIR - 1))
            sp.dma_start(ka_raw[0:HD, :], proj[ROW_KA:ROW_KA + HD, :]).then_inc(late_in, 16)
            sp.dma_start(ka_raw[HD:P, :], proj[ROW_KA:ROW_KA + HD, :]).then_inc(late_in, 16)
            sp.dma_start(sel[:, :, :], c_sel).then_inc(late_in, 16)
            sp.dma_start(bias[:, :, :], c_bias).then_inc(late_in, 16)
            sp.dma_start(sink1[:, :], sinks.broadcast_to([P, H])).then_inc(late_in, 16)
            sp.dma_start(qa_raw[:, 0, :, :], c_rhi).then_inc(late_in, 16)
            sp.dma_start(qa_raw[:, 1, :, :], c_rlo).then_inc(late_in, 16)
            sp.dma_start(qb_raw[:, 0, 0, :], c_upper).then_inc(late_in, 16)
            sp.dma_start(gate[HD:P, 0, :, :], c_extm).then_inc(late_in, 16)
            sp.dma_start(ext_raw[HD:P, :], c_extk).then_inc(late_in, 16)

            for b in range(NB):
                s = b % 2
                if b < 2:
                    sp.wait_ge(setup_act, 8)
                else:
                    sp.wait_ge(y_gated, 2 * (b - 1))
                cols = slice(P * b, P * b + P)
                for r in range(2):
                    rows = slice(HD * r, HD * r + HD)
                    sp.dma_start(qa_raw[rows, s, :, :], proj[ROW_QA:ROW_QA + H * HD, cols]
                                 .rearrange("(h d) t -> d h t", d=HD)).then_inc(block_in[s], 16)
                    sp.dma_start(qb_raw[rows, s, :, :], proj[ROW_QB:ROW_QB + H * HD, cols]
                                 .rearrange("(h d) t -> d h t", d=HD)).then_inc(block_in[s], 16)
                    j0 = HD if b == 0 else 0
                    sp.dma_start(kb_raw[rows, s, :, j0:WIN],
                                 proj[ROW_KB:ROW_KB + P, P * b - HD + j0:P * b + P]
                                 .rearrange("(g d) t -> d g t", d=HD)).then_inc(block_in[s], 16)
                sp.dma_start(gate[:, s, :, :], proj[ROW_G:ROW_G + D, cols]
                             .rearrange("(t p) n -> p t n", p=P)).then_inc(block_in[s], 16)
                if b >= 2:
                    sp.dma_start(mask[:, s, 0:P * (b + 1)], masks[b, :, 0:P * (b + 1)]) \
                        .then_inc(block_in[s], 16)

            sp.wait_ge(y_gated, 2 * NB)
            for i in range(2):
                sp.wait_ge(y_stored[i], 16 * NB // 2)
            for k in range(KT):
                sp.dma_start(wo_raw[:, k, :], w_out[:, k, :]).then_inc(wo_in, 16)
            sp.dma_start(gains[:, :], ln_g.broadcast_to([P, D])).then_inc(fin_dma, 16)
            sp.dma_start(shifts[:, :], ln_b.broadcast_to([P, D])).then_inc(fin_dma, 16)
            for b in range(NB):
                s = b % 2
                if b >= 2:
                    sp.wait_ge(o_z, b - 1)
                sp.dma_start(x_row[:, s, :], x_res[P * b:P * b + P, :]).then_inc(row_in[s], 16)
                sp.dma_start(yt_raw[:, s, :, :], y_t[:, P * b:P * b + P]
                             .rearrange("(k p) t -> p k t", p=P)).then_inc(row_in[s], 16)
            for i in range(2):
                sp.wait_ge(out_dma[i], 16 * NB // 2)

        @block.gpsimd
        def _(pool):
            nc.gpsimd.memset(vw[:, :, 64:65], 1.0).then_inc(setup_pool, 1)

            def store_masks(p):
                pool.wait_ge(mask_ok, p)
                for j in range(2):
                    pool.dma_start(masks[2 * p + j, :, 0:nd(p)], above[:, j, 0:nd(p)]).then_inc(mask_out, 16)

            def split_tiles(half, first, n):
                base = item_of(half, first)

                def body(i):
                    for u in range(2):
                        pool.wait_ge(hi_done, i * 2 + (base + u + 1))
                        nc.gpsimd.tensor_tensor(w_lo[:, u, :, :].rearrange("p k c -> p (k c)"), raw[:, u, :],
                                                w_hi[:, u, :, :].bitcast(F32).rearrange("p k c -> p (k c)"),
                                                ALU.subtract).then_inc(lo_done, 1)

                tile_pairs(pool, half * N_TILES + first, n, body)

            for half in range(2):
                base = item_of(half, 0) - KT - (2 if half == 0 else 0)
                for k in range(KT):
                    n = base + k
                    pool.wait_ge(hi_done, n + 1)
                    nc.gpsimd.tensor_tensor(x_lo[:, k, :], raw[:, n % 2, :], x_hi[:, k, :].bitcast(F32),
                                            ALU.subtract).then_inc(lo_done, 1)
                if half == 0:
                    for j in range(2):
                        n = KT + j
                        pool.wait_ge(hi_done, n + 1)
                        nc.gpsimd.tensor_tensor(
                            wn_lo[:, 4 * j:4 * j + 4, :].rearrange("p k n -> p (k n)"), raw[:, n % 2, 0:4 * VN],
                            wn_hi[:, 4 * j:4 * j + 4, :].bitcast(F32).rearrange("p k n -> p (k n)"),
                            ALU.subtract).then_inc(lo_done, 1)
                split_tiles(half, 0, KEY_TILES)
                pool.wait_ge(ki_hi_ok, half + 1)
                nc.gpsimd.tensor_tensor(ki_lo[:, half * HALF:(half + 1) * HALF], ki_raw[0:HD, :],
                                        ki_hi[0:HD, half * HALF:(half + 1) * HALF].bitcast(F32),
                                        ALU.subtract).then_inc(ki_lo_ok, 1)
                for g, (first, n, _) in enumerate(segments(half)):
                    for p in PAIRS_AT.get((half, g), []):
                        if p > 1:
                            store_masks(p - 1)
                        pool.wait_ge(qi_hi_ok, p)
                        nc.gpsimd.tensor_tensor(qi_split[HD:P, :, :], qi_raw[HD:P, :, :],
                                                qi_split[HD:P, :, :].bitcast(F32),
                                                ALU.subtract).then_inc(qi_lo_ok, 1)
                    split_tiles(half, first, n)
            store_masks(NPAIR - 1)
            pool.wait_ge(setup_act, 1)
            nc.gpsimd.tensor_tensor(ka_mix[0:HD, :], ka_raw[0:HD, :], ka_ext[0:HD, 0, :].bitcast(F32),
                                    ALU.subtract).then_inc(setup_pool, 1)
            for b in range(NB):
                s = b % 2
                if b:
                    if b >= 2:
                        pool.wait_ge(a_used, units_to(b - 2))
                    else:
                        pool.wait_ge(setup_act, 8)
                    pool.wait_ge(split, b)
                    nc.gpsimd.tensor_scalar(ka_ext[96:98, s, :], ka_ext[96:98, s, :].bitcast(F32),
                                            -float(P * min(b, 2)), None, ALU.add).then_inc(pos_ok, 1)
                    pool.wait_ge(pos_ok, b)
                pool.wait_ge(rounded, b + 1)
                nc.gpsimd.tensor_tensor(qa_mix[HD:P, s, :, :], qa_raw[HD:P, s, :, :],
                                        qa_mix[HD:P, s, :, :].bitcast(F32), ALU.subtract)
                j0 = HD if b == 0 else 0
                nc.gpsimd.tensor_tensor(kb_lo[:, s, :, j0:WIN], kb_raw[0:HD, s, :, j0:WIN],
                                        kb_hi[0:HD, s, :, j0:WIN].bitcast(F32), ALU.subtract)
                nc.gpsimd.tensor_tensor(qb_mix[HD:P, s, :, :], qb_raw[HD:P, s, :, :],
                                        qb_mix[HD:P, s, :, :].bitcast(F32), ALU.subtract)
                nc.gpsimd.memset(qa_ext[HD:HD + H, s, :, :].bitcast(F32), 0.0).then_inc(split, 1)
            pool.wait_ge(y_gated, 2 * NB)
            nc.gpsimd.memset(minus_half[:, :], -0.5).then_inc(setup_pool, 1)
            for k in range(KT):
                pool.wait_ge(wo_split, k + 1)
                nc.gpsimd.tensor_tensor(wo_lo[:, k, :], wo_raw[:, k, :], wo_hi[:, k, :].bitcast(F32),
                                        ALU.subtract).then_inc(yt_lo_ok, 1)
            pool.wait_ge(setup_pool, 3)
            for b in range(NB):
                s = b % 2
                pool.wait_ge(yt_hi_ok, b + 1)
                nc.gpsimd.tensor_tensor(yt_lo[:, s, :, :], yt_raw[:, s, :, :], yt_hi[:, s, :, :].bitcast(F32),
                                        ALU.subtract).then_inc(yt_lo_ok, 1)
                pool.wait_ge(o_var, b + 1)
                nc.gpsimd.tensor_tensor(rstd[:, :], var_eps[:, :], minus_half[:, :], ALU.pow).then_inc(o_rstd, 1)

        @block.scalar
        def _(act):
            def round_item(n, dst, src):
                act.wait_ge(raw_in[n % 2], 16 * (n // 2 + 1))
                nc.scalar.activation(dst, src, ACT.Copy).then_inc(hi_done, 1)

            def tiles(half, first, n, gated):
                g0 = half * N_TILES + first
                base = item_of(half, first)

                def body(i):
                    for u in range(2):
                        act.wait_ge(raw_in[u], i * 16 + 16 * (base // 2 + 1))
                        wait_if(act, tile_mm, i * 2 + (g0 + u - 1))
                        nc.scalar.activation(w_hi[:, u, :, :].rearrange("p k c -> p (k c)"), raw[:, u, :],
                                             ACT.Copy).then_inc(hi_done, 1)
                    for u in range(2):
                        act.wait_ge(tile_mm, i * 2 + (g0 + u + 1))
                        wait_if(act, stored[u], i * 16 + 16 * (g0 // 2))
                        nc.scalar.activation(staged[:, u, :], psum[:, 2 * u:2 * u + 2, :]
                                             .rearrange("p b n -> p (b n)"),
                                             ACT.Silu if gated else ACT.Copy).then_inc(tile_out, 1)
                    for u in range(2):
                        act.wait_ge(tile_out, i * 2 + (g0 + u + 1))
                        act.dma_start(proj_tile(i * 2 + (first + u), half), staged[:, u, :]) \
                            .then_inc(stored[u], 16)

                tile_pairs(act, g0, n, body)

            for half in range(2):
                base = item_of(half, 0) - KT - (2 if half == 0 else 0)
                if half == 1:
                    act.wait_ge(tile_mm, N_TILES)
                for k in range(KT):
                    n = base + k
                    round_item(n, x_hi[:, k, :], raw[:, n % 2, :])
                if half == 0:
                    for j in range(2):
                        round_item(KT + j, wn_hi[:, 4 * j:4 * j + 4, :].rearrange("p k n -> p (k n)"),
                                   raw[:, (KT + j) % 2, 0:4 * VN])
                tiles(half, 0, KEY_TILES, False)
                for j in range(NPAIR):
                    b = half * NPAIR + j
                    act.wait_ge(norm_mm, b + 1)
                    bank = 2 * (j % 2)
                    nc.scalar.activation(vw[:, b, 0:HD], psum[:, bank, 0:HD], ACT.Copy)
                    nc.scalar.activation(vw[:, b, HD + 1:VN + 1], psum[:, bank, HD:VN], ACT.Copy) \
                        .then_inc(norm_out, 1)
                act.wait_ge(ki_in, 32 * (half + 1))
                nc.scalar.activation(ki_hi[:, half * HALF:(half + 1) * HALF], ki_raw[:, :],
                                     ACT.Copy).then_inc(ki_hi_ok, 1)
                for g, (first, n, gated) in enumerate(segments(half)):
                    for p in PAIRS_AT.get((half, g), []):
                        act.wait_ge(qi_in, 32 * p)
                        if p > 1:
                            act.wait_ge(dots, chunks_before(p))
                        nc.scalar.activation(qi_split[:, :, :], qi_raw[:, :, :], ACT.Copy).then_inc(qi_hi_ok, 1)
                        n_chunk = chunks_before(p)
                        for j in range(2):
                            for c, w in chunks(p):
                                act.wait_ge(dots, n_chunk + 1)
                                if n_chunk:
                                    act.wait_ge(summed, IH * n_chunk)
                                nc.scalar.activation(relu[:, :, 0:w], psum[:, 4:8, 0:w], ACT.Relu,
                                                     scale=IH ** -0.5 * HD ** -0.5).then_inc(relued, 1)
                                n_chunk += 1
                    tiles(half, first, n, gated)

            act.wait_ge(late_in, 16 * 10)
            nc.scalar.activation(ka_ext[0:HD, 0, :], ka_raw[0:HD, :], ACT.Copy).then_inc(setup_act, 1)
            nc.scalar.activation(ka_ext[0:HD, 1, :], ka_raw[0:HD, :], ACT.Copy)
            nc.scalar.activation(ka_mix[HD:P, :], ka_raw[HD:P, :], ACT.Copy)
            nc.scalar.activation(r_hi[:, :, :], qa_raw[:, 0, :, :], ACT.Copy).then_inc(setup_act, 1)
            nc.scalar.activation(r_lo[:, :, :], qa_raw[:, 1, :, :], ACT.Copy).then_inc(setup_act, 1)
            nc.scalar.activation(upper[:, :], qb_raw[:, 0, 0, :], ACT.Copy).then_inc(setup_act, 1)
            for i in range(2):
                nc.scalar.activation(qa_ext[HD:P, i, :, :], gate[HD:P, 0, :, :], ACT.Copy)
                nc.scalar.activation(ka_ext[HD:P, i, :], ext_raw[HD:P, :], ACT.Copy)
            for i in range(4):
                nc.scalar.activation(ident4[:, i, :], ident[:, :], ACT.Copy)
            nc.scalar.activation(sink8[:, :], sink1[:, :], ACT.Copy, scale=8.0).then_inc(setup_act, 4)

            def round_block(b):
                s = b % 2
                act.wait_ge(block_in[s], loaded(b))
                if b >= 2:
                    act.wait_ge(a_used, units_to(b - 2))
                j0 = HD if b == 0 else 0
                nc.scalar.activation(qa_ext[0:HD, s, :, :], qa_raw[0:HD, s, :, :], ACT.Copy)
                nc.scalar.activation(qa_mix[:, s, :, :], qa_raw[:, s, :, :], ACT.Copy)
                nc.scalar.activation(qb_mix[:, s, :, :], qb_raw[:, s, :, :], ACT.Copy)
                nc.scalar.activation(kb_hi[:, s, :, j0:WIN], kb_raw[:, s, :, j0:WIN], ACT.Copy) \
                    .then_inc(rounded, 1)

            round_block(0)
            unit = 0
            for b in range(NB):
                if b + 1 < NB:
                    round_block(b + 1)
                j0 = HD if b == 0 else 0
                act.wait_ge(b_max, b + 1)
                nc.scalar.activation(ez[:, :], zb[:, :], ACT.Exp)
                for h in range(H):
                    last = nc.scalar.activation(lb[:, h, j0:WIN], lb[:, h, j0:WIN], ACT.Exp,
                                                bias=nmb[:, h:h + 1], scale=0.125, accum_out=sum_b[:, h:h + 1])
                last.then_inc(b_exp, 1)
                act.wait_ge(b_turned, b + 1)
                nc.scalar.activation(ptb_own[:, :, :].rearrange("p h q -> p (h q)"), psum[:, 4:6, :]
                                     .rearrange("p b n -> p (b n)"), ACT.Copy).then_inc(b_pt, 1)
                if b:
                    nc.scalar.activation(ptb_prev[HD:P, :, :].rearrange("p h q -> p (h q)"),
                                         psum[0:HD, 6:8, :].rearrange("p b n -> p (b n)"),
                                         ACT.Copy).then_inc(b_ptp, 1)
                for _ in range(2 * (b + 1)):
                    act.wait_ge(a_logits, unit + 1)
                    if unit >= 3:
                        act.wait_ge(a_used, unit - 2)
                    nc.scalar.activation(prob[:, unit % 3, :], psum[:, 4 + unit % 2, :], ACT.Exp,
                                         scale=0.125).then_inc(a_prob, 1)
                    unit += 1
                act.wait_ge(a_used, units_to(b))
                nc.scalar.activation(out_a[:, :, :], psum[0:65, 6:8, :], ACT.Copy).then_inc(a_outsb, 1)
                act.wait_ge(y_gated, 2 * (b + 1))
                act.dma_start(y_t[:, P * b:P * b + P].rearrange("(k p) t -> p k t", p=P),
                              yt_sb[:, b % 2, :, :]).then_inc(y_stored[b % 2], 16)

            def store_rows(b):
                act.wait_ge(o_done, b + 1)
                act.dma_start(out[P * b:P * b + P, :], z[:, b % 2, :]).then_inc(out_dma[b % 2], 16)

            act.wait_ge(y_gated, 2 * NB)
            for k in range(KT):
                act.wait_ge(wo_in, 16 * KT)
                nc.scalar.activation(wo_hi[:, k, :], wo_raw[:, k, :], ACT.Copy).then_inc(wo_split, 1)
            for b in range(NB):
                s = b % 2
                act.wait_ge(row_in[s], 32 * (b // 2 + 1))
                if b >= 2:
                    act.wait_ge(o_mm, b - 1)
                nc.scalar.activation(yt_hi[:, s, :, :], yt_raw[:, s, :, :], ACT.Copy).then_inc(yt_hi_ok, 1)
                if b:
                    store_rows(b - 1)
            store_rows(NB - 1)

        @block.tensor
        def _(pe):
            def tiles(half, first, n):
                g0 = half * N_TILES + first
                base = item_of(half, first)

                def body(i):
                    for u in range(2):
                        pe.wait_ge(lo_done, i * 2 + (base + u + 1))
                        wait_if(pe, tile_out, i * 2 + (g0 + u - 1))
                        for m in range(2):
                            cols = slice(512 * m, 512 * m + 512)
                            for k in range(KT):
                                for q, (wt, xt) in enumerate(((w_hi, x_hi), (w_hi, x_lo), (w_lo, x_hi))):
                                    last = pe.matmul(psum[:, 2 * u + m, :], wt[:, u, k, :], xt[:, k, cols],
                                                     start=(k == 0 and q == 0), stop=(k == KT - 1 and q == 2))
                        last.then_inc(tile_mm, 1)

                tile_pairs(pe, g0, n, body)

            def normal_form(half):
                pe.wait_ge(tile_out, half * N_TILES + KEY_TILES)
                for j in range(NPAIR):
                    b = half * NPAIR + j
                    if j >= 2:
                        pe.wait_ge(norm_out, b - 1)
                    toks = slice(P * j, P * j + P)
                    for k in range(KT):
                        for q, (xt, wt) in enumerate(((x_hi, wn_hi), (x_hi, wn_lo), (x_lo, wn_hi))):
                            last = pe.matmul(psum[:, 2 * (j % 2), 0:VN], xt[:, k, toks], wt[:, k, :],
                                             start=(k == 0 and q == 0), stop=(k == KT - 1 and q == 2))
                    last.then_inc(norm_mm, 1)
                pe.wait_ge(norm_out, NPAIR * (half + 1))

            def index_dots(p):
                pe.wait_ge(qi_lo_ok, p)
                n_chunk = chunks_before(p)
                for j in range(2):
                    for c, w in chunks(p):
                        if n_chunk:
                            pe.wait_ge(relued, n_chunk)
                        for h in range(IH):
                            pe.matmul(psum[:, 4 + h, 0:w], qi_split[:, h, P * j:P * j + P],
                                      ki_hi[:, c:c + w], start=True, stop=False)
                            last = pe.matmul(psum[:, 4 + h, 0:w], qi_split[0:HD, h, P * j:P * j + P],
                                             ki_lo[:, c:c + w], start=False, stop=True)
                        last.then_inc(dots, 1)
                        n_chunk += 1

            for half in range(2):
                tiles(half, 0, KEY_TILES)
                normal_form(half)
                pe.wait_ge(ki_lo_ok, half + 1)
                for g, (first, n, _) in enumerate(segments(half)):
                    for p in PAIRS_AT.get((half, g), []):
                        index_dots(p)
                    tiles(half, first, n)

            pe.wait_ge(tile_out, 2 * N_TILES)
            pe.wait_ge(relued, chunks_before(NPAIR))
            pe.wait_ge(setup_act, 8)
            pe.wait_ge(setup_pool, 2)
            unit = 0
            scan = 0
            for b in range(NB):
                s = b % 2
                j0 = HD if b == 0 else 0
                keys = P * (b + 1)
                pe.wait_ge(split, b + 1)
                if b == 0:
                    pe.wait_ge(setup_dve, 1)
                else:
                    pe.wait_ge(y_gated, 2 * b)
                for h in range(H):
                    o = psum[:, h // 2, WIN * (h % 2) + j0:WIN * (h % 2) + WIN]
                    pe.matmul(o, qb_mix[:, s, h, :], kb_hi[:, s, h // 4, j0:WIN], start=True, stop=False)
                    last = pe.matmul(o, qb_mix[0:HD, s, h, :], kb_lo[:, s, h // 4, j0:WIN],
                                     start=False, stop=True)
                last.then_inc(b_logits, 1)
                pe.wait_ge(b_biased, b + 1)
                if b:
                    pe.wait_ge(pos_ok, b)
                for h in range(H):
                    for c in range(0, keys, 1024):
                        if scan >= 2:
                            pe.wait_ge(a_scanned, scan - 1)
                        for k0 in range(c, min(c + 1024, keys), 512):
                            w = min(512, keys - k0)
                            bank = 2 * (scan % 2) + (k0 - c) // 512
                            diag = k0 + w == keys
                            last = pe.matmul(psum[:, bank, 0:w], qa_ext[:, s, h, :], ka_ext[:, s, k0:k0 + w],
                                             start=True, stop=not diag)
                            if diag:
                                last = pe.matmul(psum[:, bank, w - P:w], r_hi[:, h, :], upper[:, :],
                                                 start=False, stop=True)
                        last.then_inc(a_scan, 1)
                        scan += 1
                pe.wait_ge(b_exp, b + 1)
                for h in range(H):
                    last = pe.transpose(psum[:, 4 + h // 4, P * (h % 4):P * (h % 4) + P], lb[:, h, HD:WIN],
                                        ident[:, :])
                    if b:
                        last = pe.transpose(psum[0:HD, 6 + h // 4, P * (h % 4):P * (h % 4) + P],
                                            lb[:, h, 0:HD], ident[:, :])
                last.then_inc(b_turned, 1)
                pe.wait_ge(a_neg, b + 1)
                pe.transpose(psum[0:H, 1, 0:P], neg_max[:, :], ident[:, :]).then_inc(a_negt, 1)
                pe.wait_ge(b_pt, b + 1)
                if b:
                    pe.wait_ge(b_ptp, b)
                for h in range(H):
                    o = psum[:, 0, HD * h:HD * h + HD]
                    v0 = HD + 1 + HD * (h // 4)
                    if b:
                        pe.matmul(o, ptb_prev[HD:P, h, :], vw[HD:P, b - 1, v0:v0 + HD], start=True, stop=False)
                    last = pe.matmul(o, ptb_own[:, h, :], vw[:, b, v0:v0 + HD], start=(b == 0), stop=True)
                last.then_inc(b_mixed, 1)
                pe.wait_ge(a_ext, b + 1)

                def logits(u, kt, g):
                    if u >= 2:
                        pe.wait_ge(a_prob, u - 1)
                    o = psum[:, 4 + u % 2, :]
                    ks = slice(P * kt, P * kt + P)
                    hs = slice(4 * g, 4 * g + 4)
                    flat = lambda t: t.rearrange("p h q -> p (h q)")
                    pe.matmul(o, mask[:, s, ks], flat(ident4[:, :, :]), start=True, stop=False)
                    pe.matmul(o, ka_mix[:, ks], flat(qa_mix[:, s, hs, :]), start=False, stop=False)
                    last = pe.matmul(o, ka_ext[:, s, ks], flat(qa_ext[:, s, hs, :]), start=False, stop=(kt < b))
                    if kt == b:
                        pe.matmul(o, upper[:, :], flat(r_hi[:, hs, :]), start=False, stop=False)
                        last = pe.matmul(o, upper[:, :], flat(r_lo[:, hs, :]), start=False, stop=True)
                    last.then_inc(a_logits, 1)

                units = [(kt, g) for kt in range(b + 1) for g in range(2)]
                logits(unit, *units[0])
                for n, (kt, g) in enumerate(units):
                    if n + 1 < len(units):
                        logits(unit + 1, *units[n + 1])
                    pe.wait_ge(a_prob, unit + 1)
                    last = pe.matmul(psum[0:65, 6 + g, :], vw[:, kt, 0:65], prob[:, unit % 3, :],
                                     start=(kt == 0), stop=(kt == b)).then_inc(a_used, 1)
                    unit += 1
                pe.wait_ge(a_outsb, b + 1)
                for h in range(H):
                    last = pe.transpose(psum[:, 2 + h // 4, 65 * (h % 4):65 * (h % 4) + 65],
                                        out_a[:, h // 4, P * (h % 4):P * (h % 4) + P], ident[0:65, 0:65])
                last.then_inc(a_turned, 1)
                pe.wait_ge(b_y, b + 1)
                for t in range(4):
                    last = pe.transpose(psum[:, 0, P * t:P * t + P],
                                        y_b[:, 2 * t:2 * t + 2, :].rearrange("p h d -> p (h d)"), ident[:, :])
                last.then_inc(y_turned, 1)
                pe.wait_ge(a_y, b + 1)
                for t in range(4):
                    last = pe.transpose(psum[:, 1, P * t:P * t + P],
                                        y_a[:, 2 * t:2 * t + 2, :].rearrange("p h d -> p (h d)"), ident[:, :])
                last.then_inc(y_turned, 1)

            pe.wait_ge(y_gated, 2 * NB)
            for b in range(NB):
                s = b % 2
                pe.wait_ge(yt_lo_ok, KT + b + 1)
                if b >= 2:
                    pe.wait_ge(o_z, b - 1)
                for m in range(2):
                    cols = slice(512 * m, 512 * m + 512)
                    for k in range(KT):
                        for q, (yt, wt) in enumerate(((yt_hi, wo_hi), (yt_hi, wo_lo), (yt_lo, wo_hi))):
                            last = pe.matmul(psum[:, 2 * s + m, :], yt[:, s, k, :], wt[:, k, cols],
                                             start=(k == 0 and q == 0), stop=(k == KT - 1 and q == 2))
                last.then_inc(o_mm, 1)

        @block.vector
        def _(dve):
            v = nc.vector
            n_prep = 0
            n_trial = 0
            n_count = 0
            n_sum = 0
            dve.wait_ge(const_in, 32)
            for p in range(1, NPAIR):
                n = nd(p)
                if p > 1:
                    dve.wait_ge(mask_out, 32 * (p - 1))
                n_chunk = chunks_before(p)
                for j in range(2):
                    b = 2 * p + j
                    for c, w in chunks(p):
                        dve.wait_ge(relued, n_chunk + 1)
                        dve.wait_ge(norm_out, b + 1)
                        o = score[:, j, c:c + w]
                        for h in range(IH):
                            wt = vw[:, b, VN + 1 - IH + h:VN + 2 - IH + h]
                            if h == 0:
                                v.tensor_scalar(o, relu[:, h, 0:w], wt, 0.0, ALU.mult, ALU.add) \
                                    .then_inc(summed, 1)
                            else:
                                dve.wait_ge(summed, n_sum)
                                v.scalar_tensor_tensor(o, relu[:, h, 0:w], wt, o, ALU.mult, ALU.add) \
                                    .then_inc(summed, 1)
                            n_sum += 1
                        n_chunk += 1
                dve.wait_ge(summed, n_sum)
                low = -3.0e38
                v.memset(score[0:HD, 0, n - P - HD:n - P], low)
                v.memset(score[0:HD, 1, n - HD:n], low)
                v.memset(score[:, 0, n - P:n], low).then_inc(prep, 1)
                n_prep += 1
                dve.wait_ge(prep, n_prep)
                sc = score[:, :, 0:n].bitcast(I32)
                di = dist[:, :, 0:n].bitcast(I32)
                v.tensor_scalar(di, sc, 31, 0x7fffffff, ALU.arith_shift_right, ALU.bitwise_and) \
                    .then_inc(prep, 1)
                dve.wait_ge(prep, n_prep + 1)
                v.tensor_tensor(sc, sc, di, ALU.bitwise_xor).then_inc(prep, 1)
                dve.wait_ge(prep, n_prep + 2)
                v.tensor_scalar(di, sc, -65536, None, ALU.bitwise_and).then_inc(prep, 1)
                n_prep += 3
                for part in range(2):
                    u = trial[:, part, :]
                    if part == 0:
                        v.memset(u, -32768.0).then_inc(trial_ok, 1)
                    else:
                        dve.wait_ge(trial_ok, n_trial)
                        for j in range(2):
                            lows = score[:, j, 0:n].bitcast(U16).rearrange("p (n t) -> p n t", t=2)[:, :, 0]
                            v.scalar_tensor_tensor(dist[:, j, 0:n], dist[:, j, 0:n].bitcast(I32),
                                                   trial[:, 0, j:j + 1], lows, ALU.subtract, ALU.add)
                        v.memset(u, 32767.5).then_inc(trial_ok, 1)
                    n_trial += 1
                    dve.wait_ge(prep, n_prep)
                    with dve.Fori(0, 16) as i:
                        dve.wait_ge(trial_ok, i + n_trial)
                        for j in range(2):
                            src = dist[:, j, 0:n].bitcast(I32) if part == 0 else dist[:, j, 0:n]
                            last = v.tensor_scalar(above[:, j, 0:n], src, u[:, j:j + 1], None, ALU.is_ge,
                                                   ALU.add, accum_out=count[:, j:j + 1])
                        last.then_inc(counted, 1)
                        dve.wait_ge(counted, i + (n_count + 1))
                        v.tensor_scalar(accept[:, :], count[:, :], float(TOPK), 0.5, ALU.is_ge, ALU.subtract) \
                            .then_inc(accepted, 1)
                        dve.wait_ge(accepted, i + (n_count + 1))
                        v.scalar_tensor_tensor(u, accept[:, :], steps[:, bass.ds(i + 16 * part, 1)], u,
                                               ALU.mult, ALU.add).then_inc(trial_ok, 1)
                    n_trial += 16
                    n_count += 16
                dve.wait_ge(trial_ok, n_trial)
                for j in range(2):
                    t = trial[:, 1, j:j + 1]
                    v.tensor_scalar(above[:, j, 0:n], dist[:, j, 0:n], t, None, ALU.is_gt, ALU.add,
                                    accum_out=n_above[:, j:j + 1])
                    v.tensor_scalar(equal[:, j, 0:n], dist[:, j, 0:n], t, None, ALU.is_equal).then_inc(prep, 1)
                n_prep += 2
                dve.wait_ge(prep, n_prep)
                for j in range(2):
                    v.tensor_tensor_scan(score[:, j, 0:n], equal[:, j, 0:n], equal[:, j, 0:n],
                                         n_above[:, j:j + 1], ALU.add, ALU.max).then_inc(prep, 1)
                n_prep += 2
                dve.wait_ge(prep, n_prep)
                v.scalar_tensor_tensor(equal[:, :, 0:n], score[:, :, 0:n], float(TOPK), equal[:, :, 0:n],
                                       ALU.is_le, ALU.mult).then_inc(prep, 1)
                n_prep += 1
                dve.wait_ge(prep, n_prep)
                v.scalar_tensor_tensor(above[:, :, 0:n], equal[:, :, 0:n], -1.0, above[:, :, 0:n],
                                       ALU.add, ALU.add).then_inc(prep, 1)
                n_prep += 1
                dve.wait_ge(prep, n_prep)
                v.tensor_scalar(above[:, :, 0:n], above[:, :, 0:n], BIG, None, ALU.mult).then_inc(mask_ok, 1)

            dve.wait_ge(mask_out, 32 * (NPAIR - 1))
            for i in range(2):
                dve.wait_ge(stored[i], 16 * N_TILES)
            v.memset(mask[:, 0, 0:P], 0.0)
            v.memset(mask[:, 1, 0:2 * P], 0.0).then_inc(prep, 1)
            n_prep += 1
            dve.wait_ge(prep, n_prep)
            v.memset(mask[0:HD, 0, HD:P], -BIG)
            v.memset(mask[0:HD, 1, P + HD:2 * P], -BIG).then_inc(setup_dve, 1)
            dve.wait_ge(setup_act, 8)
            n_step = 0
            scan = 0
            for b in range(NB):
                s = b % 2
                j0 = HD if b == 0 else 0
                keys = P * (b + 1)
                dve.wait_ge(b_logits, b + 1)
                if b:
                    dve.wait_ge(b_turned, b)
                ps = psum[:, 0:4, 0:2 * WIN].rearrange("p b (h j) -> p b h j", h=2)[:, :, :, j0:WIN]
                four = lambda t: t[:, :, :].rearrange("p (b h) j -> p b h j", h=2)[:, :, :, j0:WIN]
                v.tensor_tensor(four(lb), ps, four(bias), ALU.add).then_inc(b_biased, 1)
                dve.wait_ge(b_biased, b + 1)
                v.tensor_reduce(mb[:, :], lb[:, :, j0:WIN], AX_X, ALU.max).then_inc(b_step, 1)
                dve.wait_ge(b_step, n_step + 1)
                v.tensor_tensor(mb2[:, :], mb[:, :], sink8[:, :], ALU.max).then_inc(b_step, 1)
                dve.wait_ge(b_step, n_step + 2)
                v.tensor_scalar(nmb[:, :], mb2[:, :], -0.125, None, ALU.mult).then_inc(b_step, 1)
                dve.wait_ge(b_step, n_step + 3)
                n_step += 3
                v.tensor_tensor(zb[:, :], nmb[:, :], sink1[:, :], ALU.add).then_inc(b_max, 1)
                if b >= 2:
                    dve.wait_ge(block_in[s], loaded(b))
                for h in range(H):
                    for ci, c in enumerate(range(0, keys, 1024)):
                        w = min(1024, keys - c)
                        dve.wait_ge(a_scan, scan + 1)
                        if scan >= 2:
                            dve.wait_ge(a_scanned, scan - 1)
                        src = psum[:, 2 * (scan % 2):2 * (scan % 2) + 2, :].rearrange("p b n -> p (b n)")[:, 0:w]
                        v.tensor_tensor_reduce(out=junk[:, scan % 2, 0:w], in0=src, in1=mask[:, s, c:c + w], scale=1.0,
                                               scalar=-3.0e38, op0=ALU.add, op1=ALU.max,
                                               accum_out=part_max[:, ci, h:h + 1]).then_inc(a_scanned, 1)
                        scan += 1
                dve.wait_ge(a_scanned, scan)
                if keys > 1024:
                    v.tensor_tensor(neg_max[:, :], part_max[:, 0, :], part_max[:, 1, :], ALU.max) \
                        .then_inc(b_step, 1)
                    n_step += 1
                    dve.wait_ge(b_step, n_step)
                    v.tensor_scalar(neg_max[:, :], neg_max[:, :], -1.0, None, ALU.mult).then_inc(a_neg, 1)
                else:
                    v.tensor_scalar(neg_max[:, :], part_max[:, 0, :], -1.0, None, ALU.mult).then_inc(a_neg, 1)
                dve.wait_ge(a_negt, b + 1)
                v.tensor_tensor(qa_ext[HD:HD + H, s, :, :], psum[0:H, 1, 0:P].unsqueeze(1).broadcast_to([H, H, P]),
                                sel[:, :, :], ALU.mult).then_inc(a_ext, 1)
                dve.wait_ge(b_exp, b + 1)
                v.tensor_tensor(den_b[:, :], sum_b[:, :], ez[:, :], ALU.add).then_inc(b_step, 1)
                dve.wait_ge(b_step, n_step + 1)
                v.reciprocal(rec_b[:, :], den_b[:, :]).then_inc(b_step, 1)
                dve.wait_ge(b_step, n_step + 2)
                n_step += 2
                dve.wait_ge(b_mixed, b + 1)
                v.tensor_tensor(y_b[:, :, :], psum[:, 0, :].rearrange("p (h d) -> p h d", h=H),
                                rec_b[:, :].unsqueeze(2).broadcast_to([P, H, HD]), ALU.mult).then_inc(b_y, 1)
                dve.wait_ge(a_turned, b + 1)
                heads = [psum[:, 2 + g, 0:4 * 65].rearrange("p (h d) -> p h d", h=4) for g in range(2)]
                for g in range(2):
                    last = v.reciprocal(rec_a[:, 4 * g:4 * g + 4], heads[g][:, :, HD])
                last.then_inc(a_rec, 1)
                dve.wait_ge(a_rec, b + 1)
                for g in range(2):
                    last = v.tensor_tensor(y_a[:, 4 * g:4 * g + 4, :], heads[g][:, :, 0:HD],
                                           rec_a[:, 4 * g:4 * g + 4].unsqueeze(2).broadcast_to([P, 4, HD]),
                                           ALU.mult)
                last.then_inc(a_y, 1)
                if b >= 2:
                    dve.wait_ge(y_stored[s], 16 * (b // 2))
                dve.wait_ge(block_in[s], loaded(b))
                for g, bank in ((1, 0), (0, 1)):
                    dve.wait_ge(y_turned, 2 * b + 2 - g)
                    v.tensor_tensor(yt_sb[:, s, 4 * g:4 * g + 4, :].rearrange("p t q -> p (t q)"),
                                    psum[:, bank, :],
                                    gate[:, s, 4 * g:4 * g + 4, :].rearrange("p t q -> p (t q)"),
                                    ALU.mult).then_inc(y_gated, 1)

            dve.wait_ge(fin_dma, 32)
            n_o = 0
            for b in range(NB):
                s = b % 2
                dve.wait_ge(o_mm, b + 1)
                dve.wait_ge(row_in[s], 32 * (b // 2 + 1))
                if b >= 2:
                    dve.wait_ge(out_dma[s], 16 * (b // 2))
                v.scalar_tensor_tensor(z[:, s, :], x_row[:, s, :], ALPHA, psum[:, 2 * s:2 * s + 2, :]
                                       .rearrange("p b n -> p (b n)"), ALU.mult, ALU.add).then_inc(o_z, 1)
                dve.wait_ge(o_z, b + 1)
                for m in range(2):
                    last = v.bn_stats(stats[:, m, :], z[:, s, 512 * m:512 * m + 512])
                last.then_inc(o_step, 1)
                dve.wait_ge(o_step, n_o + 1)
                v.bn_aggr(moments[:, :], stats[:, :, :]).then_inc(o_step, 1)
                dve.wait_ge(o_step, n_o + 2)
                v.tensor_scalar(var_eps[:, :], moments[:, 1:2], EPS, None, ALU.add).then_inc(o_var, 1)
                dve.wait_ge(o_rstd, b + 1)
                v.tensor_scalar(z[:, s, :], z[:, s, :], moments[:, 0:1], rstd[:, 0:1], ALU.subtract, ALU.mult) \
                    .then_inc(o_step, 1)
                dve.wait_ge(o_step, n_o + 3)
                v.tensor_tensor(z[:, s, :], z[:, s, :], gains[:, :], ALU.mult).then_inc(o_step, 1)
                dve.wait_ge(o_step, n_o + 4)
                v.tensor_tensor(z[:, s, :], z[:, s, :], shifts[:, :], ALU.add).then_inc(o_done, 1)
                n_o += 4

def shape_constants():
    slopes = np.array([2.0 ** (-8.0 * (i + 1) / (2 * H)) for i in range(2 * H)], np.float32)
    sa, sbl = slopes[0::2] * np.float32(8), slopes[1::2] * np.float32(8)
    bits = sa.view(np.uint32)
    sa_hi = ((bits + np.uint32(0x7FF) + ((bits >> np.uint32(12)) & np.uint32(1))) & np.uint32(0xFFFFF000)).view(np.float32)
    sa_lo = sa - sa_hi
    eye = np.eye(P, dtype=np.float32)
    q = np.arange(P)
    upper = np.maximum(q[None, :] - q[:, None], 0).astype(np.float32)
    r_hi = np.stack([-2 * s * eye for s in sa_hi], 1)
    r_lo = np.stack([-2 * s * eye for s in sa_lo], 1)
    extm = np.zeros((P - HD, H, P), np.float32)
    extm[32] = sa_hi[:, None]
    extm[33] = sa_lo[:, None]
    extk = np.zeros((P - HD, L), np.float32)
    extk[0:H] = 1.0
    extk[32:34] = np.arange(L)
    j = np.arange(WIN)
    dist = np.abs(q[:, None] + HD - j[None, :]).astype(np.float32)
    seen = np.where(q[:, None] < HD, j[None, :] < P, j[None, :] >= HD)
    bias = np.where(seen[:, None, :], -sbl[None, :, None] * dist[:, None, :], np.float32(-BIG)).astype(np.float32)
    sel = np.repeat(np.eye(H, dtype=np.float32)[:, :, None], P, 2)
    steps = np.repeat(np.array([2.0 ** (31 - i) for i in range(32)], np.float32)[None], P, 0)
    return dict(c_step=steps, c_ident=eye, c_upper=upper, c_rhi=r_hi, c_rlo=r_lo, c_extm=extm,
                c_extk=extk, c_bias=bias, c_sel=sel)

def kernel(**inputs):
    import concourse.bacc as bacc
    from concourse.bass_utils import run_bass_kernel_spmd

    nc = bacc.Bacc("TRN2", target_bir_lowering=False, num_devices=1)
    x = np.ascontiguousarray(inputs["x"])[0]
    w = np.ascontiguousarray(inputs["w_in"])[0]
    order = np.r_[1152:1408, 1408:1472, 512:576, 1988:2116, 0:512, 1476:1988, 640:1152, 2244:2756]
    w_tiles = w[:, order].reshape(KT, P, N_TILES, P).transpose(2, 1, 0, 3).reshape(N_TILES, P, KT * P)
    w_norm = w[:, np.r_[576:640, 2116:2244, 1472:1476]].reshape(KT, P, VN).transpose(1, 0, 2)
    w_out = np.asarray(inputs["w_out"])[0].reshape(KT, P, D).transpose(1, 0, 2)
    arrays = dict(xT=x.T, w_tiles=w_tiles, w_norm=w_norm, w_out=w_out, x_res=x,
                  sinks=np.asarray(inputs["sinks"]), ln_g=np.asarray(inputs["ln_g"]),
                  ln_b=np.asarray(inputs["ln_b"]), **shape_constants())
    arrays = {k: np.ascontiguousarray(a) for k, a in arrays.items()}
    args = {k: nc.dram_tensor(k, a.shape, F32, kind="ExternalInput").ap() for k, a in arrays.items()}
    args["proj"] = nc.dram_tensor("proj", (N_TILES * P, L), F32, kind="Internal").ap()
    args["masks"] = nc.dram_tensor("masks", (NB, P, L), BF16, kind="Internal").ap()
    args["y_t"] = nc.dram_tensor("y_t", (D, L), F32, kind="Internal").ap()
    args["out"] = nc.dram_tensor("out", (1, L, D), F32, kind="ExternalOutput").ap().rearrange("a l d -> (a l) d")
    hybrid_kernel(nc, **args)
    r = run_bass_kernel_spmd(nc, [arrays], core_ids=[0])
    return r.results[0]["out"]
```

```python
from contextlib import ExitStack

import numpy as np

import concourse.bass as bass
from concourse import mybir

F32 = mybir.dt.float32
F32R = mybir.dt.float32r
BF16 = mybir.dt.bfloat16
I32 = mybir.dt.int32
U16 = mybir.dt.uint16
I16 = mybir.dt.int16
ALU = mybir.AluOpType
ACT = mybir.ActivationFunctionType
AX_X = mybir.AxisListType.X

P = 128
L = 2048
D = 1024
KT = D // P
NB = L // P
NPAIR = NB // 2
HALF = L // 2
H = 8
HD = 64
IH = 4
TOPK = 256
BIG = float(2.0 ** 100)
N_TILES = 20
KEY_TILES = 4
VN = 196
WIN = 192
ROW_QI, ROW_KI, ROW_KA, ROW_KB, ROW_QA, ROW_QB, ROW_G = 0, 256, 320, 384, 512, 1024, 1536
ALPHA = 2.0 ** 0.25
EPS = 1e-5

PLAN = [("keys", 0, None), ("index", 1), ("tiles", 0, 4, 4, False, (1, 2)),
        ("index", 2), ("tiles", 0, 8, 4, False, (2, 1)), ("tiles", 0, 12, 4, True, (2, 1)),
        ("index", 3), ("tiles", 0, 16, 4, True, (3, 1)), ("keys", 1, (3, 1)),
        ("index", 4), ("tiles", 1, 4, 8, False, (4, 1)),
        ("index", 5), ("tiles", 1, 12, 8, True, (5, 1))]
INDEX_AT = {0: 6, 6: 7}
SEARCH_AT = {1: (6, 0, 1), 2: (6, 1, 1), 3: (6, 2, 2), 4: (6, 4, 2), 5: (6, 6, 2),
             7: (7, 0, 1), 8: (7, 1, 1), 9: (7, 2, 2), 10: (7, 4, 2), 11: (7, 6, 2)}


def attention_step(b):
    pieces = []
    if b >= 2:
        pieces += [(("turn_a", b - 2), 2.0), (("columns_a", b - 2), 1.5)]
    if b < NB:
        pieces.append((("window", b), 3.0))
        searches = []
        if b in SEARCH_AT:
            pair, first, n = SEARCH_AT[b]
            searches = [("search", pair, first + i) for i in range(n)]
        for h in range(H):
            pieces.append((("scan", b, h), 0.6))
            if h >= 2:
                pieces.append((("exp_b", b, h - 2), 0.0))
            if searches and h in (3, 6):
                pieces.append((searches.pop(0), 10.0))
        pieces += [(("exp_b", b, H - 2), 0.0), (("exp_b", b, H - 1), 0.5), (("turn_b", b), 2.5),
                   (("minus_max", b), 1.0), (("mix_b", b), 1.0)]
        if b + 1 < NB:
            pieces.append((("next_b", b + 1), 0.5))
        pieces.append((("columns_b", b), 0.5))
        if b in SEARCH_AT and SEARCH_AT[b][1] + SEARCH_AT[b][2] == 8:
            pieces.append((("masks", SEARCH_AT[b][0]), 6.0))
    if b in INDEX_AT:
        pair = INDEX_AT[b]
        pieces.append((("index", pair), 0.5))
        n = 2 * P * (pair + 1)
        for j in range(2):
            for c in range(0, n, 512):
                pieces.append((("dots", pair, j, c, min(512, n - c)), 1.0))
        pieces.append((("sortable", pair), 6.0))
    units = [("unit", b - 1, kt, g) for kt in range(b) for g in range(2)] if 1 <= b <= NB else []
    total, so_far, placed, order = sum(w for _, w in pieces), 0.0, 0, []
    for piece, weight in pieces:
        order.append(piece)
        so_far += weight
        upto = round(len(units) * so_far / total)
        order += units[placed:upto]
        placed = max(placed, upto)
    order += units[placed:]
    if units:
        order.append(("leave_a", b - 1))
    if b + 1 < NB:
        order.append(("next_a", b + 1))
    if b in (NB - 2, NB - 1):
        order += [("w_out", k) for k in range(4 * (b - NB + 2), 4 * (b - NB + 3))]
    return order


def run_steps(engine_pieces):
    for b in range(NB + 2):
        for kind, *what in attention_step(b):
            if kind in engine_pieces:
                engine_pieces[kind](*what)


def hybrid_kernel(nc, xT, w_tiles, w_norm, w_out, x_res, sinks, ln_g, ln_b, c_step, c_ident,
                  c_upper, c_pow, c_extm, c_extk, c_bias, c_sel, proj, masks, y_t, out):
    with ExitStack() as ctx:
        def sem(name):
            return ctx.enter_context(nc.semaphore(name))

        def sb(stack, name, shape, dt):
            return stack.enter_context(nc.sbuf_tensor(name, shape, dt))

        psum = ctx.enter_context(nc.psum_tensor("psum", [P, 8, 512], F32))

        vw = sb(ctx, "vw", [P, NB, 200], F32)
        ident = sb(ctx, "ident", [P, P], F32)
        steps = sb(ctx, "steps", [P, 32], F32)
        trial = sb(ctx, "trial", [P, 2, 2], F32)
        count = sb(ctx, "count", [P, 2], F32)
        accept = sb(ctx, "accept", [P, 2], F32)
        n_above = sb(ctx, "n_above", [P, 2], F32)
        with ExitStack() as topk:
            ki_hi = sb(topk, "ki_hi", [P, L], F32R)
            ki_lo = sb(topk, "ki_lo", [HD, L], F32R)
            qi_raw = sb(topk, "qi_raw", [P, IH, 2 * P], F32)
            qi_split = sb(topk, "qi_split", [P, IH, 2 * P], F32R)
            relu = sb(topk, "relu", [P, IH, 512], F32)
            score = sb(topk, "score", [P, 2, L], F32)
            dist = sb(topk, "dist", [P, 2, L], F32)
            above = sb(topk, "above", [P, 2, L], BF16)
            half_rows = score[:, :, :].bitcast(BF16)
            equal = half_rows[:, :, 0:L]
            rank = score[:, :, :].bitcast(I16)[:, :, L:2 * L]
            with ExitStack() as early:
                x_hi = sb(early, "x_hi", [P, KT, HALF], F32R)
                x_lo = sb(early, "x_lo", [P, KT, HALF], F32R)
                raw = sb(early, "raw", [P, 2, KT * P], F32)
                w_hi = sb(early, "w_hi", [P, 2, KT, P], F32R)
                w_lo = sb(early, "w_lo", [P, 2, KT, P], F32R)
                wn_hi = sb(early, "wn_hi", [P, KT, VN], F32R)
                wn_lo = sb(early, "wn_lo", [P, KT, VN], F32R)
                staged = sb(early, "staged", [P, 2, HALF], F32)
                ki_raw = sb(early, "ki_raw", [P, HALF], F32)
            with ExitStack() as late:
                ka_ext = sb(late, "ka_ext", [P, 2, L], F32R)
                ka_mix = sb(late, "ka_mix", [P, L], F32R)
                qa_raw = sb(late, "qa_raw", [P, H, P], F32)
                qb_raw = sb(late, "qb_raw", [P, H, P], F32)
                kb_raw = sb(late, "kb_raw", [P, 2, WIN], F32)
                gate_a = sb(late, "gate_a", [P, 4, P], F32)
                gate_b = sb(late, "gate_b", [P, 4, P], F32)
                mask = sb(late, "mask", [P, 2, L], BF16)
                qa_ext = sb(late, "qa_ext", [P, 2, H, P], F32R)
                qa_mix = sb(late, "qa_mix", [P, 2, H, P], F32R)
                qb_mix = sb(late, "qb_mix", [P, H, P], F32R)
                kb_hi = sb(late, "kb_hi", [P, 2, WIN], F32R)
                kb_lo = sb(late, "kb_lo", [HD, 2, WIN], F32R)
                upper = sb(late, "upper", [P, 2, P], F32R)
                power = sb(late, "power", [P, H, P], F32R)
                ident4 = sb(late, "ident4", [P, 4, P], BF16)
                sel = sb(late, "sel", [H, H, P], BF16)
                bias = sb(late, "bias", [P, H, WIN], F32)
                lb = sb(late, "lb", [P, H, WIN], F32)
                ptb_own = sb(late, "ptb_own", [P, H, P], F32)
                ptb_prev = sb(late, "ptb_prev", [P, H, P], F32)
                prob = sb(late, "prob", [P, 3, 512], F32)
                out_a = sb(late, "out_a", [65, 2, 512], F32)
                y_a = sb(late, "y_a", [P, H, HD], F32)
                y_b = sb(late, "y_b", [P, H, HD], F32)
                yt_a = sb(late, "yt_a", [P, 4, P], F32)
                yt_b = sb(late, "yt_b", [P, 4, P], F32)
                junk = sb(late, "junk", [P, 2, 1024], BF16)
                part_max = sb(late, "part_max", [P, 2, H], F32)
                neg_max = sb(late, "neg_max", [P, H], F32)
                sink8 = sb(late, "sink8", [P, H], F32)
                sink1 = sb(late, "sink1", [P, H], F32)
                mb = sb(late, "mb", [P, H], F32)
                mb2 = sb(late, "mb2", [P, H], F32)
                nmb = sb(late, "nmb", [P, H], F32)
                zb = sb(late, "zb", [P, H], F32)
                ez = sb(late, "ez", [P, H], F32)
                sum_b = sb(late, "sum_b", [P, H], F32)
                den_b = sb(late, "den_b", [P, H], F32)
                rec_b = sb(late, "rec_b", [P, H], F32)
                rec_a = sb(late, "rec_a", [P, H], F32)
        with ExitStack() as last:
            wo_raw = sb(last, "wo_raw", [P, 2, D], F32)
            wo_hi = sb(last, "wo_hi", [P, KT, D], F32R)
            wo_lo = sb(last, "wo_lo", [P, KT, D], F32R)
            yt_raw = sb(last, "yt_raw", [P, 2, KT, P], F32)
            yt_hi = sb(last, "yt_hi", [P, 2, KT, P], F32R)
            yt_lo = sb(last, "yt_lo", [P, 2, KT, P], F32R)
            x_row = sb(last, "x_row", [P, 2, D], F32)
            z = sb(last, "z", [P, 3, D], F32)
            gains = sb(last, "gains", [P, D], F32)
            shifts = sb(last, "shifts", [P, D], F32)
            stats = sb(last, "stats", [P, 2, 6], F32)
            moments = sb(last, "moments", [P, 2, 2], F32)
            var_eps = sb(last, "var_eps", [P, 2], F32)
            minus_half = sb(last, "minus_half", [P, 1], F32)
            rstd = sb(last, "rstd", [P, 2], F32)

        raw_in = [sem(f"raw_in{i}") for i in range(2)]
        hi_done = sem("hi_done")
        lo_done = sem("lo_done")
        x_used = sem("x_used")
        tile_mm = sem("tile_mm")
        tile_out = sem("tile_out")
        stored = [sem(f"stored{i}") for i in range(2)]
        norm_mm = sem("norm_mm")
        norm_out = sem("norm_out")
        const_in = sem("const_in")
        ki_in = sem("ki_in")
        ki_hi_ok = sem("ki_hi_ok")
        ki_lo_ok = sem("ki_lo_ok")
        qi_in = sem("qi_in")
        qi_hi_ok = sem("qi_hi_ok")
        qi_lo_ok = sem("qi_lo_ok")
        dots = sem("dots")
        relued = sem("relued")
        summed = sem("summed")
        trial_ok = sem("trial_ok")
        counted = sem("counted")
        signed = sem("signed")
        accepted = sem("accepted")
        prep = sem("prep")
        mask_ok = sem("mask_ok")
        mask_out = sem("mask_out")
        stage_in = [sem(f"stage_in{i}") for i in range(3)]
        staged_ok = [sem(f"staged_ok{i}") for i in range(3)]
        late_in = sem("late_in")
        setup_act = sem("setup_act")
        setup_pool = sem("setup_pool")
        setup_dve = sem("setup_dve")
        qa_in = sem("qa_in")
        qb_in = sem("qb_in")
        gate_a_in = sem("gate_a_in")
        gate_b_in = sem("gate_b_in")
        mask_in = [sem(f"mask_in{i}") for i in range(2)]
        qa_round = sem("qa_round")
        qb_round = sem("qb_round")
        qa_zero = sem("qa_zero")
        qa_split = sem("qa_split")
        qb_split = sem("qb_split")
        pos_ok = sem("pos_ok")
        b_logits = sem("b_logits")
        b_biased = sem("b_biased")
        b_step = sem("b_step")
        b_max = sem("b_max")
        b_exp = sem("b_exp")
        b_turned = sem("b_turned")
        b_pt = sem("b_pt")
        b_mixed = sem("b_mixed")
        b_y = sem("b_y")
        b_yt = sem("b_yt")
        b_gated = sem("b_gated")
        b_stored = sem("b_stored")
        a_scan = sem("a_scan")
        a_scanned = sem("a_scanned")
        a_neg = sem("a_neg")
        a_negt = sem("a_negt")
        a_ext = sem("a_ext")
        a_logits = sem("a_logits")
        a_prob = sem("a_prob")
        a_used = sem("a_used")
        a_outsb = sem("a_outsb")
        a_turned = sem("a_turned")
        a_rec = sem("a_rec")
        a_y = sem("a_y")
        a_yt = sem("a_yt")
        a_gated = sem("a_gated")
        a_stored = sem("a_stored")
        wo_in = [sem(f"wo_in{i}") for i in range(2)]
        wo_hi_ok = sem("wo_hi_ok")
        wo_lo_ok = sem("wo_lo_ok")
        row_in = [sem(f"row_in{i}") for i in range(2)]
        yt_hi_ok = sem("yt_hi_ok")
        yt_lo_ok = sem("yt_lo_ok")
        o_mm = sem("o_mm")
        o_z = sem("o_z")
        o_step = sem("o_step")
        o_var = sem("o_var")
        o_rstd = sem("o_rstd")
        o_done = sem("o_done")
        out_dma = [sem(f"out_dma{i}") for i in range(3)]
        ln_in = sem("ln_in")

        HALF_ITEM = [0, N_TILES + KT + 2]

        def item_of(half, tile):
            return HALF_ITEM[half] + tile + (KT if tile >= 1 else 0) + (2 if half == 0 and tile >= 2 else 0)

        def tile_ahead(half, first, n):
            return first + 2, min(n, N_TILES - 2 - first)

        def units_to(b):
            return (b + 1) * (b + 2)

        def scans_to(b):
            return H * sum(1 + (i >= 8) for i in range(b + 1))

        def nd(p):
            return 2 * P * (p + 1)

        def chunks(p):
            return [(c, min(512, nd(p) - c)) for c in range(0, nd(p), 512)]

        def chunks_before(p):
            return sum(2 * len(chunks(i)) for i in range(1, p))

        def tile_pairs(engine, g0, n, body):
            if g0 == 0 or n <= 2:
                for i in range(n // 2):
                    body(i)
            else:
                with engine.Fori(0, n // 2) as i:
                    body(i)

        def wait_if(engine, s, value):
            if not (isinstance(value, int) and value <= 0):
                engine.wait_ge(s, value)

        def proj_tile(tile, half):
            return proj.rearrange("(t p) n -> t p n", p=P)[bass.ds(tile, 1), :, half * HALF:(half + 1) * HALF] \
                .rearrange("a p n -> p (a n)")

        def flat(t):
            return t.rearrange("p h q -> p (h q)")

        x_view = xT.rearrange("(k p) t -> k p t", p=P)
        block = ctx.enter_context(nc.Block())

        @block.sync
        def _(sp):
            sp.dma_start(ident[:, :], c_ident).then_inc(const_in, 16)
            sp.dma_start(steps[:, :], c_step).then_inc(const_in, 16)

            def load_tiles(half, first, n):
                first, n = tile_ahead(half, first, n)
                base = item_of(half, first)

                def body(i):
                    for u in range(2):
                        sp.wait_ge(lo_done, i * 2 + (base + u - 1))
                        sp.dma_start(raw[:, u, :], w_tiles[bass.ds(i * 2 + (first + u), 1), :, :]
                                     .rearrange("a p n -> p (a n)")).then_inc(raw_in[u], 16)

                tile_pairs(sp, first, n, body)

            def load_item(n, src, width):
                if n >= 2:
                    sp.wait_ge(lo_done, n - 1)
                sp.dma_start(raw[:, n % 2, 0:width], src).then_inc(raw_in[n % 2], 16)

            def load_index(p):
                for i in range(2):
                    sp.wait_ge(stored[i], 16 * (p // 4 * N_TILES // 2 + 1))
                if p > 1:
                    sp.wait_ge(qi_lo_ok, p - 1)
                for r in range(2):
                    sp.dma_start(qi_raw[HD * r:HD * r + HD, :, :],
                                 proj[ROW_QI:ROW_QI + IH * HD, 2 * P * p:2 * P * p + 2 * P]
                                 .rearrange("(h d) t -> d h t", d=HD)).then_inc(qi_in, 16)

            def load_keys(half):
                load_item(item_of(half, 0), w_tiles[0], KT * P)
                for k in range(KT):
                    load_item(item_of(half, 0) + 1 + k, x_view[k, :, half * HALF:(half + 1) * HALF], HALF)
                load_item(item_of(half, 1), w_tiles[1], KT * P)
                if half == 0:
                    for j in range(2):
                        load_item(item_of(0, 1) + 1 + j,
                                  w_norm[:, 4 * j:4 * j + 4, :].rearrange("p k n -> p (k n)"), 4 * VN)
                load_tiles(half, 0, KEY_TILES)

            for kind, *what in PLAN:
                if kind == "keys":
                    load_keys(what[0])
                elif kind == "index":
                    load_index(*what)
                else:
                    load_tiles(*what[:3])

            for i in range(2):
                sp.wait_ge(stored[i], 16 * N_TILES)
            sp.wait_ge(ki_lo_ok, 2)
            sp.dma_start(bias[:, :, :], c_bias).then_inc(late_in, 16)
            sp.dma_start(sink1[:, :], sinks.broadcast_to([P, H])).then_inc(late_in, 16)
            for i in range(2):
                if i:
                    sp.wait_ge(staged_ok[0], 1)
                for r in range(2):
                    sp.dma_start(qa_raw[HD * r:HD * r + HD, :, :].rearrange("p h q -> p (h q)"),
                                 proj[ROW_KA:ROW_KA + HD, HALF * i:HALF * (i + 1)]).then_inc(stage_in[0], 16)
            sp.dma_start(flat(qb_raw[HD:P, :, :]), c_extk[:, 0:HALF]).then_inc(stage_in[1], 16)
            sp.dma_start(gate_a[HD:P, :, :], c_extm[:, 0:4, :]).then_inc(stage_in[2], 16)
            sp.dma_start(gate_b[HD:P, :, :], c_extm[:, 4:8, :]).then_inc(stage_in[2], 16)
            sp.wait_ge(staged_ok[1], 1)
            sp.dma_start(flat(qb_raw[HD:P, :, :]), c_extk[:, HALF:L]).then_inc(stage_in[1], 16)
            sp.wait_ge(staged_ok[0], 2)
            sp.dma_start(qa_raw[:, :, :], c_pow).then_inc(stage_in[0], 16)
            sp.wait_ge(staged_ok[1], 2)
            sp.dma_start(qb_raw[:, 0:2, :], c_upper).then_inc(stage_in[1], 16)
            sp.wait_ge(staged_ok[2], 1)
            sp.dma_start(gate_a[0:H, :, :], c_sel[:, 0:4, :]).then_inc(stage_in[2], 16)
            sp.dma_start(gate_b[0:H, :, :], c_sel[:, 4:8, :]).then_inc(stage_in[2], 16)
            sp.wait_ge(setup_act, 1)

            def load_qa(b):
                if b:
                    sp.wait_ge(qa_split, b)
                for r in range(2):
                    sp.dma_start(qa_raw[HD * r:HD * r + HD, :, :], proj[ROW_QA:ROW_QA + H * HD, P * b:P * b + P]
                                 .rearrange("(h d) t -> d h t", d=HD)).then_inc(qa_in, 16)

            def load_qb(b):
                if b:
                    sp.wait_ge(qb_split, b)
                j0 = HD if b == 0 else 0
                for r in range(2):
                    rows = slice(HD * r, HD * r + HD)
                    sp.dma_start(qb_raw[rows, :, :], proj[ROW_QB:ROW_QB + H * HD, P * b:P * b + P]
                                 .rearrange("(h d) t -> d h t", d=HD)).then_inc(qb_in, 16)
                    sp.dma_start(kb_raw[rows, :, j0:WIN], proj[ROW_KB:ROW_KB + P, P * b - HD + j0:P * b + P]
                                 .rearrange("(g d) t -> d g t", d=HD)).then_inc(qb_in, 16)

            def load_gate(t, row, b, s):
                sp.dma_start(t[:, :, :], proj[row:row + 4 * P, P * b:P * b + P]
                             .rearrange("(t p) n -> p t n", p=P)).then_inc(s, 16)

            load_qb(0)
            load_qa(0)
            load_gate(gate_b, ROW_G + 4 * P, 0, gate_b_in)
            for b in range(NB + 2):
                if 2 <= b < NB:
                    sp.wait_ge(mask_out, 32 * (b // 2))
                    sp.wait_ge(a_used, units_to(b - 2))
                    sp.dma_start(mask[:, b % 2, 0:P * (b + 1)], masks[b, :, 0:P * (b + 1)]) \
                        .then_inc(mask_in[b % 2], 16)
                if b in INDEX_AT:
                    load_index(INDEX_AT[b])
                if b + 1 < NB:
                    load_qb(b + 1)
                    load_qa(b + 1)
                if 0 < b < NB:
                    sp.wait_ge(b_gated, b)
                    load_gate(gate_b, ROW_G + 4 * P, b, gate_b_in)
                if 1 <= b <= NB:
                    if b >= 2:
                        sp.wait_ge(a_gated, b - 1)
                    load_gate(gate_a, ROW_G, b - 1, gate_a_in)
                if b in (NB - 2, NB - 1):
                    sp.wait_ge(mask_out, 32 * (NPAIR - 1))
                    for k in range(4 * (b - NB + 2), 4 * (b - NB + 3)):
                        if k >= 2:
                            sp.wait_ge(wo_lo_ok, k - 1)
                        sp.dma_start(wo_raw[:, k % 2, :], w_out[:, k, :]).then_inc(wo_in[k % 2], 16)

            sp.wait_ge(a_gated, NB)
            sp.wait_ge(a_stored, 16 * NB)
            sp.wait_ge(b_stored, 16 * NB)
            sp.dma_start(gains[:, :], ln_g.broadcast_to([P, D])).then_inc(ln_in, 16)
            sp.dma_start(shifts[:, :], ln_b.broadcast_to([P, D])).then_inc(ln_in, 16)
            for b in range(NB):
                s = b % 2
                if b >= 2:
                    sp.wait_ge(o_z, b - 1)
                sp.dma_start(x_row[:, s, :], x_res[P * b:P * b + P, :]).then_inc(row_in[s], 16)
                sp.dma_start(yt_raw[:, s, :, :], y_t[:, P * b:P * b + P]
                             .rearrange("(k p) t -> p k t", p=P)).then_inc(row_in[s], 16)
            for i in range(3):
                sp.wait_ge(out_dma[i], 16 * len(range(i, NB, 3)))

        @block.gpsimd
        def _(pool):
            nc.gpsimd.memset(vw[:, :, 64:65], 1.0).then_inc(setup_pool, 1)

            def store_masks(p):
                pool.wait_ge(mask_ok, p)
                for j in range(2):
                    pool.dma_start(masks[2 * p + j, :, 0:nd(p)], above[:, j, 0:nd(p)]).then_inc(mask_out, 16)

            def split_tile(n, u):
                pool.wait_ge(hi_done, n + 1)
                nc.gpsimd.tensor_tensor(w_lo[:, u, :, :].rearrange("p k c -> p (k c)"), raw[:, u, :],
                                        w_hi[:, u, :, :].bitcast(F32).rearrange("p k c -> p (k c)"),
                                        ALU.subtract).then_inc(lo_done, 1)

            def split_tiles(half, first, n):
                first, n = tile_ahead(half, first, n)
                base = item_of(half, first)

                def body(i):
                    for u in range(2):
                        split_tile(i * 2 + (base + u), u)

                tile_pairs(pool, first, n, body)

            def split_index(p, items):
                pool.wait_ge(lo_done, items)
                pool.wait_ge(qi_hi_ok, p)
                nc.gpsimd.tensor_tensor(qi_split[HD:P, :, :], qi_raw[HD:P, :, :],
                                        qi_split[HD:P, :, :].bitcast(F32), ALU.subtract).then_inc(qi_lo_ok, 1)
                pool.wait_ge(qi_lo_ok, p)

            def split_keys(half):
                split_tile(item_of(half, 0), 0)
                for k in range(KT):
                    n = item_of(half, 0) + 1 + k
                    pool.wait_ge(hi_done, n + 1)
                    nc.gpsimd.tensor_tensor(x_lo[:, k, :], raw[:, n % 2, :], x_hi[:, k, :].bitcast(F32),
                                            ALU.subtract).then_inc(lo_done, 1)
                split_tile(item_of(half, 1), 1)
                if half == 0:
                    for j in range(2):
                        n = item_of(0, 1) + 1 + j
                        pool.wait_ge(hi_done, n + 1)
                        nc.gpsimd.tensor_tensor(
                            wn_lo[:, 4 * j:4 * j + 4, :].rearrange("p k n -> p (k n)"), raw[:, n % 2, 0:4 * VN],
                            wn_hi[:, 4 * j:4 * j + 4, :].bitcast(F32).rearrange("p k n -> p (k n)"),
                            ALU.subtract).then_inc(lo_done, 1)
                split_tiles(half, 0, KEY_TILES)
                pool.wait_ge(ki_hi_ok, half + 1)
                nc.gpsimd.tensor_tensor(ki_lo[:, half * HALF:(half + 1) * HALF], ki_raw[0:HD, :],
                                        ki_hi[0:HD, half * HALF:(half + 1) * HALF].bitcast(F32),
                                        ALU.subtract).then_inc(ki_lo_ok, 1)

            items = 0
            for kind, *what in PLAN:
                if kind == "keys":
                    split_keys(what[0])
                    items = item_of(what[0], KEY_TILES + 2)
                elif kind == "index":
                    if what[0] > 1:
                        store_masks(what[0] - 1)
                    split_index(what[0], items)
                else:
                    split_tiles(*what[:3])
                    items = item_of(what[0], min(what[1] + what[2] + 2, N_TILES))

            for i in range(2):
                pool.wait_ge(setup_pool, 1 + i)
                pool.wait_ge(setup_dve, 1 + i)
                nc.gpsimd.tensor_tensor(ka_mix[0:HD, HALF * i:HALF * (i + 1)], flat(qa_raw[0:HD, :, :]),
                                        ka_ext[0:HD, 0, HALF * i:HALF * (i + 1)].bitcast(F32),
                                        ALU.subtract).then_inc(setup_pool, 1)
                pool.wait_ge(setup_pool, 2 + i)
                nc.gpsimd.memset(neg_max[:, :], 0.0).then_inc(staged_ok[0], 1)

            def split_qb(b):
                j0 = HD if b == 0 else 0
                pool.wait_ge(qb_round, b + 1)
                nc.gpsimd.tensor_tensor(kb_lo[:, :, j0:WIN], kb_raw[0:HD, :, j0:WIN],
                                        kb_hi[0:HD, :, j0:WIN].bitcast(F32), ALU.subtract)
                nc.gpsimd.tensor_tensor(qb_mix[HD:P, :, :], qb_raw[HD:P, :, :],
                                        qb_mix[HD:P, :, :].bitcast(F32), ALU.subtract).then_inc(qb_split, 1)

            def split_qa(b):
                s = b % 2
                if b >= 2:
                    pool.wait_ge(a_used, units_to(b - 2))
                else:
                    pool.wait_ge(setup_act, 1)
                nc.gpsimd.memset(qa_ext[HD:HD + H, s, :, :].bitcast(F32), 0.0).then_inc(qa_zero, 1)
                pool.wait_ge(qa_round, b + 1)
                nc.gpsimd.tensor_tensor(qa_mix[HD:P, s, :, :], qa_raw[HD:P, :, :],
                                        qa_mix[HD:P, s, :, :].bitcast(F32), ALU.subtract).then_inc(qa_split, 1)

            def store_a(b):
                pool.wait_ge(a_gated, b + 1)
                pool.dma_start(y_t[0:4 * P, P * b:P * b + P].rearrange("(k p) t -> p k t", p=P),
                               yt_a[:, :, :]).then_inc(a_stored, 16)

            def store_b(b):
                pool.wait_ge(b_gated, b + 1)
                pool.dma_start(y_t[4 * P:D, P * b:P * b + P].rearrange("(k p) t -> p k t", p=P),
                               yt_b[:, :, :]).then_inc(b_stored, 16)

            def index(p):
                if p == 6:
                    store_masks(5)
                split_index(p, items)

            def split_w_out(k):
                if k == 0:
                    pool.wait_ge(qa_split, NB)
                pool.wait_ge(wo_hi_ok, k + 1)
                nc.gpsimd.tensor_tensor(wo_lo[:, k, :], wo_raw[:, k % 2, :], wo_hi[:, k, :].bitcast(F32),
                                        ALU.subtract).then_inc(wo_lo_ok, 1)
                if k == 3:
                    pool.wait_ge(wo_lo_ok, 4)

            split_qb(0)
            split_qa(0)
            run_steps({"index": index, "columns_a": store_a, "columns_b": store_b,
                       "next_b": split_qb, "next_a": split_qa, "masks": store_masks, "w_out": split_w_out})
            pool.wait_ge(a_gated, NB)
            nc.gpsimd.memset(minus_half[:, :], -0.5).then_inc(setup_pool, 1)
            pool.wait_ge(setup_pool, 4)
            for b in range(NB + 1):
                if b < NB:
                    s = b % 2
                    pool.wait_ge(yt_hi_ok, b + 1)
                    nc.gpsimd.tensor_tensor(yt_lo[:, s, :, :], yt_raw[:, s, :, :],
                                            yt_hi[:, s, :, :].bitcast(F32), ALU.subtract).then_inc(yt_lo_ok, 1)
                if b:
                    s = (b - 1) % 2
                    pool.wait_ge(o_var, b)
                    nc.gpsimd.tensor_tensor(rstd[:, s:s + 1], var_eps[:, s:s + 1], minus_half[:, :],
                                            ALU.pow).then_inc(o_rstd, 1)

        @block.scalar
        def _(act):
            done = {"count": 0}

            def copy(dst, src, **kw):
                return nc.scalar.activation(dst, src, ACT.Copy, **kw)

            def round_item(n, dst, src):
                act.wait_ge(raw_in[n % 2], 16 * (n // 2 + 1))
                copy(dst, src).then_inc(hi_done, 1)

            def round_tile(n, u):
                act.wait_ge(raw_in[u], n)
                nc.scalar.activation(w_hi[:, u, :, :].rearrange("p k c -> p (k c)"), raw[:, u, :],
                                     ACT.Copy).then_inc(hi_done, 1)

            def evacuate(g, u, gated):
                act.wait_ge(tile_mm, g + 1)
                wait_if(act, stored[u], 16 * (g // 2) if isinstance(g, int) else (g - u) * 8)
                nc.scalar.activation(staged[:, u, :], psum[:, 2 * u:2 * u + 2, :].rearrange("p b n -> p (b n)"),
                                     ACT.Silu if gated else ACT.Copy).then_inc(tile_out, 1)

            def store(g, tile, half, u):
                act.wait_ge(tile_out, g + 1)
                act.dma_start(proj_tile(tile, half), staged[:, u, :]).then_inc(stored[u], 16)

            def tiles(half, first, n, gated, searching):
                for t in range(first, first + n):
                    g, u = half * N_TILES + t, t % 2
                    evacuate(g, u, gated)
                    if t + 2 < N_TILES:
                        round_tile(16 * (item_of(half, t + 2) // 2 + 1), u)
                    elif (half, t) == (0, N_TILES - 2):
                        begin_half(1)
                    store(g, t, half, u)
                    search_tile(searching)

            def search_tile(searching):
                if searching:
                    pair, n = searching
                    for _ in range(n):
                        count_steps(pair, done["count"] % 32 // 4)

            def count_steps(p, eighth):
                n = nd(p)
                part = eighth // 4
                src = dist[:, 1, 0:n].bitcast(I32) if part == 0 else dist[:, 1, 0:n]
                for _ in range(4):
                    act.wait_ge(trial_ok, done["count"] + 2 * (p - 1) + 1 + part)
                    nc.scalar.activation(above[:, 1, 0:n], src, ACT.Sign, scale=-1.0, bias=trial[:, part, 1:2],
                                         accum_out=count[:, 1:2]).then_inc(signed, 1)
                    done["count"] += 1

            def begin_half(half):
                round_tile(16 * (item_of(half, 0) // 2 + 1), 0)
                for k in range(KT):
                    if half == 1:
                        act.wait_ge(*((x_used, k + 1) if k < KT - 1 else (tile_mm, N_TILES)))
                    n = item_of(half, 0) + 1 + k
                    round_item(n, x_hi[:, k, :], raw[:, n % 2, :])

            def keys(half, searching):
                if half == 0:
                    begin_half(0)
                round_tile(16 * (item_of(half, 1) // 2 + 1), 1)
                if half == 0:
                    for j in range(2):
                        round_item(item_of(0, 1) + 1 + j, wn_hi[:, 4 * j:4 * j + 4, :].rearrange("p k n -> p (k n)"),
                                   raw[:, j, 0:4 * VN])
                tiles(half, 0, KEY_TILES, False, searching)
                act.wait_ge(stored[0], 16 * (half * N_TILES // 2 + 2))
                if half == 1:
                    act.wait_ge(ki_lo_ok, 1)
                for r in range(2):
                    act.dma_start(ki_raw[HD * r:HD * r + HD, :],
                                  proj[ROW_KI:ROW_KI + HD, half * HALF:(half + 1) * HALF]).then_inc(ki_in, 16)
                for j in range(NPAIR):
                    b = half * NPAIR + j
                    act.wait_ge(norm_mm, b + 1)
                    bank = 2 * (j % 2)
                    copy(vw[:, b, 0:HD], psum[:, bank, 0:HD])
                    copy(vw[:, b, HD + 1:VN + 1], psum[:, bank, HD:VN]).then_inc(norm_out, 1)
                act.wait_ge(ki_in, 32 * (half + 1))
                copy(ki_hi[:, half * HALF:(half + 1) * HALF], ki_raw[:, :]).then_inc(ki_hi_ok, 1)

            def index(p):
                act.wait_ge(qi_in, 32 * p)
                if p > 1:
                    act.wait_ge(dots, 2 * chunks_before(p))
                copy(qi_split[:, :, :], qi_raw[:, :, :]).then_inc(qi_hi_ok, 1)

            def index_relu(p, j, c, w, bank0):
                n_dots = 2 * (chunks_before(p) + j * len(chunks(p)) + c // 512)
                for h in (0, 2):
                    act.wait_ge(dots, n_dots + 1)
                    if n_dots >= 2:
                        act.wait_ge(summed, 2 * (n_dots - 1))
                    nc.scalar.activation(relu[:, h:h + 2, 0:w], psum[:, bank0 + h:bank0 + h + 2, 0:w], ACT.Relu,
                                         scale=IH ** -0.5 * HD ** -0.5).then_inc(relued, 1)
                    n_dots += 1

            def whole_index(p):
                index(p)
                for j in range(2):
                    for c, w in chunks(p):
                        index_relu(p, j, c, w, 4)

            for kind, *what in PLAN:
                {"keys": keys, "index": whole_index, "tiles": tiles}[kind](*what)

            for i in range(2):
                ks = slice(HALF * i, HALF * (i + 1))
                act.wait_ge(stage_in[0], 32 * (i + 1))
                copy(ka_ext[0:HD, 0, ks], flat(qa_raw[0:HD, :, :]))
                copy(ka_ext[0:HD, 1, ks], flat(qa_raw[0:HD, :, :]))
                copy(ka_mix[HD:P, ks], flat(qa_raw[HD:P, :, :])).then_inc(setup_dve, 1)
                act.wait_ge(stage_in[1], 16 * (i + 1))
                copy(ka_ext[HD:P, 0, ks], flat(qb_raw[HD:P, :, :]))
                copy(ka_ext[HD:P, 1, ks], flat(qb_raw[HD:P, :, :])).then_inc(staged_ok[1], 1)
            act.wait_ge(stage_in[2], 32)
            for i in range(2):
                copy(qa_ext[HD:P, i, 0:4, :], gate_a[HD:P, :, :])
                last = copy(qa_ext[HD:P, i, 4:8, :], gate_b[HD:P, :, :])
            last.then_inc(staged_ok[2], 1)
            act.wait_ge(stage_in[0], 80)
            copy(power[:, :, :], qa_raw[:, :, :])
            act.wait_ge(stage_in[1], 48)
            copy(upper[:, :, :], qb_raw[:, 0:2, :])
            act.wait_ge(stage_in[2], 64)
            copy(sel[:, 0:4, :], gate_a[0:H, :, :])
            copy(sel[:, 4:8, :], gate_b[0:H, :, :])
            act.wait_ge(late_in, 32)
            for i in range(4):
                copy(ident4[:, i, :], ident[:, :])
            copy(sink8[:, :], sink1[:, :], scale=8.0).then_inc(setup_act, 1)

            def round_qb(b):
                j0 = HD if b == 0 else 0
                act.wait_ge(qb_in, 64 * (b + 1))
                if b:
                    act.wait_ge(b_logits, b)
                copy(qb_mix[:, :, :], qb_raw[:, :, :])
                copy(kb_hi[:, :, j0:WIN], kb_raw[:, :, j0:WIN]).then_inc(qb_round, 1)

            def round_qa(b):
                s = b % 2
                act.wait_ge(qa_in, 32 * (b + 1))
                if b >= 2:
                    act.wait_ge(a_used, units_to(b - 2))
                copy(qa_ext[0:HD, s, :, :], qa_raw[0:HD, :, :])
                copy(qa_mix[:, s, :, :], qa_raw[:, :, :]).then_inc(qa_round, 1)

            round_qb(0)
            round_qa(0)
            def exp_b(b, h):
                j0 = HD if b == 0 else 0
                if h == 0:
                    act.wait_ge(b_max, b + 1)
                    nc.scalar.activation(ez[:, :], zb[:, :], ACT.Exp)
                last = nc.scalar.activation(lb[:, h, j0:WIN], lb[:, h, j0:WIN], ACT.Exp, bias=nmb[:, h:h + 1],
                                            scale=0.125, accum_out=sum_b[:, h:h + 1])
                if h == H - 1:
                    last.then_inc(b_exp, 1)

            def turn_b(b):
                act.wait_ge(b_turned, b + 1)
                if b:
                    act.wait_ge(b_mixed, b)
                    copy(flat(ptb_prev[HD:P, :, :]), psum[0:HD, 2:4, :].rearrange("p b n -> p (b n)"))
                copy(flat(ptb_own[:, :, :]), psum[:, 0:2, :].rearrange("p b n -> p (b n)")).then_inc(b_pt, 1)

            def exp_a(b, kt, g):
                unit = units_to(b - 1) + 2 * kt + g
                act.wait_ge(a_logits, unit + 1)
                if unit >= 3:
                    act.wait_ge(a_used, unit - 2)
                nc.scalar.activation(prob[:, unit % 3, :], psum[:, 4 + unit % 2, :], ACT.Exp,
                                     scale=0.125).then_inc(a_prob, 1)

            def leave_a(b):
                act.wait_ge(a_used, units_to(b))
                if b:
                    act.wait_ge(a_turned, b)
                copy(out_a[:, :, :], psum[0:65, 6:8, :]).then_inc(a_outsb, 1)

            def round_w_out(k):
                act.wait_ge(wo_in[k % 2], 16 * (k // 2 + 1))
                copy(wo_hi[:, k, :], wo_raw[:, k % 2, :]).then_inc(wo_hi_ok, 1)

            run_steps({"index": index, "dots": lambda p, j, c, w: index_relu(p, j, c, w, 0), "exp_b": exp_b,
                       "turn_b": turn_b, "next_b": round_qb, "unit": exp_a, "leave_a": leave_a,
                       "next_a": round_qa, "w_out": round_w_out, "search": count_steps})

            def store_rows(b):
                act.wait_ge(o_done, b + 1)
                act.dma_start(out[P * b:P * b + P, :], z[:, b % 3, :]).then_inc(out_dma[b % 3], 16)

            for b in range(NB):
                s = b % 2
                act.wait_ge(row_in[s], 32 * (b // 2 + 1))
                if b >= 2:
                    act.wait_ge(o_mm, b - 1)
                copy(yt_hi[:, s, :, :], yt_raw[:, s, :, :]).then_inc(yt_hi_ok, 1)
                if b >= 2:
                    store_rows(b - 2)
            store_rows(NB - 2)
            store_rows(NB - 1)

        @block.tensor
        def _(pe):
            def tile_products(g, n, u, x_items=None, x_last=False):
                pe.wait_ge(lo_done, n + 1)
                wait_if(pe, tile_out, g - 1)
                for k in range(KT):
                    if x_items is not None:
                        pe.wait_ge(lo_done, x_items + k + 1)
                    for m in range(2):
                        for q, (wt, xt) in enumerate(((w_hi, x_hi), (w_hi, x_lo), (w_lo, x_hi))):
                            last = pe.matmul(psum[:, 2 * u + m, :], wt[:, u, k, :], xt[:, k, 512 * m:512 * m + 512],
                                             start=(k == 0 and q == 0), stop=(k == KT - 1 and q == 2))
                    if x_last and k < KT - 1:
                        last.then_inc(x_used, 1)
                last.then_inc(tile_mm, 1)

            def tiles(half, first, n):
                g0 = half * N_TILES + first
                base = item_of(half, first)
                if first == 0:
                    for u in range(2):
                        tile_products(g0 + u, item_of(half, u), u, item_of(half, 0) + 1 if u == 0 else None)
                    g0, base, n = g0 + 2, item_of(half, 2), n - 2
                ends_x = half == 0 and first + n == N_TILES
                if ends_x:
                    n -= 2

                def body(i):
                    for u in range(2):
                        tile_products(i * 2 + (g0 + u), i * 2 + (base + u), u)

                tile_pairs(pe, g0, n, body)
                if ends_x:
                    for u in range(2):
                        tile_products(N_TILES - 2 + u, item_of(0, N_TILES - 2 + u), u, None, x_last=(u == 1))

            def keys(half):
                tiles(half, 0, KEY_TILES)
                pe.wait_ge(tile_out, half * N_TILES + KEY_TILES)
                for j in range(NPAIR):
                    b = half * NPAIR + j
                    if j >= 2:
                        pe.wait_ge(norm_out, b - 1)
                    toks = slice(P * j, P * j + P)
                    for k in range(KT):
                        for q, (xt, wt) in enumerate(((x_hi, wn_hi), (x_hi, wn_lo), (x_lo, wn_hi))):
                            last = pe.matmul(psum[:, 2 * (j % 2), 0:VN], xt[:, k, toks], wt[:, k, :],
                                             start=(k == 0 and q == 0), stop=(k == KT - 1 and q == 2))
                    last.then_inc(norm_mm, 1)
                pe.wait_ge(norm_out, NPAIR * (half + 1))
                pe.wait_ge(ki_lo_ok, half + 1)

            def index_dots(p, j, c, w, bank0):
                n_dots = 2 * (chunks_before(p) + j * len(chunks(p)) + c // 512)
                for h0 in (0, 2):
                    if n_dots >= 2:
                        pe.wait_ge(relued, n_dots - 1)
                    for h in range(h0, h0 + 2):
                        pe.matmul(psum[:, bank0 + h, 0:w], qi_split[:, h, P * j:P * j + P],
                                  ki_hi[:, c:c + w], start=True, stop=False)
                        last = pe.matmul(psum[:, bank0 + h, 0:w], qi_split[0:HD, h, P * j:P * j + P],
                                         ki_lo[:, c:c + w], start=False, stop=True)
                    last.then_inc(dots, 1)
                    n_dots += 1

            def whole_index(p):
                pe.wait_ge(qi_lo_ok, p)
                for j in range(2):
                    for c, w in chunks(p):
                        index_dots(p, j, c, w, 4)

            for kind, *what in PLAN:
                if kind == "keys":
                    keys(what[0])
                elif kind == "index":
                    whole_index(what[0])
                else:
                    tiles(*what[:3])

            pe.wait_ge(tile_out, 2 * N_TILES)
            pe.wait_ge(setup_act, 1)
            pe.wait_ge(setup_pool, 3)

            def window_logits(b):
                j0 = HD if b == 0 else 0
                pe.wait_ge(qb_split, b + 1)
                if b - 1 in INDEX_AT:
                    pe.wait_ge(relued, 2 * chunks_before(INDEX_AT[b - 1] + 1))
                if b >= 2:
                    pe.wait_ge(a_gated, b - 1)
                if b:
                    pe.wait_ge(b_gated, b)
                for h in range(H):
                    o = psum[:, h // 2, WIN * (h % 2) + j0:WIN * (h % 2) + WIN]
                    pe.matmul(o, qb_mix[:, h, :], kb_hi[:, h // 4, j0:WIN], start=True, stop=False)
                    last = pe.matmul(o, qb_mix[0:HD, h, :], kb_lo[:, h // 4, j0:WIN], start=False, stop=True)
                last.then_inc(b_logits, 1)

            def max_logits(b, h):
                s = b % 2
                n_keys = P * (b + 1)
                if h == 0:
                    pe.wait_ge(qa_round, b + 1)
                    pe.wait_ge(qa_zero, b + 1)
                    pe.wait_ge(b_biased, b + 1)
                    if b:
                        pe.wait_ge(pos_ok, b)
                scan = scans_to(b - 1) + h * (1 + (b >= 8))
                for c in range(0, n_keys, 1024):
                    if scan >= 2:
                        pe.wait_ge(a_scanned, scan - 1)
                    for k0 in range(c, min(c + 1024, n_keys), 512):
                        w = min(512, n_keys - k0)
                        bank = 2 * (scan % 2) + (k0 - c) // 512
                        diag = k0 + w == n_keys
                        last = pe.matmul(psum[:, bank, 0:w], qa_ext[:, s, h, :], ka_ext[:, s, k0:k0 + w],
                                         start=True, stop=not diag)
                        if diag:
                            last = pe.matmul(psum[:, bank, w - P:w], power[:, h, :], upper[:, 0, :],
                                             start=False, stop=True)
                    last.then_inc(a_scan, 1)
                    scan += 1

            def turn_b(b):
                pe.wait_ge(b_exp, b + 1)
                pe.wait_ge(a_scanned, scans_to(b))
                for h in range(H):
                    last = pe.transpose(psum[:, h // 4, P * (h % 4):P * (h % 4) + P], lb[:, h, HD:WIN],
                                        ident[:, :])
                    if b:
                        last = pe.transpose(psum[0:HD, 2 + h // 4, P * (h % 4):P * (h % 4) + P],
                                            lb[:, h, 0:HD], ident[:, :])
                last.then_inc(b_turned, 1)

            def minus_max(b):
                pe.wait_ge(a_neg, b + 1)
                pe.wait_ge(b_pt, b + 1)
                pe.transpose(psum[0:H, 1, 0:P], neg_max[:, :], ident[:, :]).then_inc(a_negt, 1)

            def mix_b(b):
                for h in range(H):
                    o = psum[:, 0, HD * h:HD * h + HD]
                    v0 = HD + 1 + HD * (h // 4)
                    if b:
                        pe.matmul(o, ptb_prev[HD:P, h, :], vw[HD:P, b - 1, v0:v0 + HD], start=True, stop=False)
                    last = pe.matmul(o, ptb_own[:, h, :], vw[:, b, v0:v0 + HD], start=(b == 0), stop=True)
                last.then_inc(b_mixed, 1)

            def unit_logits(b, kt, g):
                s = b % 2
                u = units_to(b - 1) + 2 * kt + g
                if u >= 2:
                    pe.wait_ge(a_prob, u - 1)
                o = psum[:, 4 + u % 2, :]
                ks = slice(P * kt, P * kt + P)
                hs = slice(4 * g, 4 * g + 4)
                pe.matmul(o, mask[:, s, ks], flat(ident4[:, :, :]), start=True, stop=False)
                pe.matmul(o, ka_mix[:, ks], flat(qa_mix[:, s, hs, :]), start=False, stop=False)
                last = pe.matmul(o, ka_ext[:, s, ks], flat(qa_ext[:, s, hs, :]), start=False, stop=(kt < b))
                if kt == b:
                    pe.matmul(o, upper[:, 0, :], flat(power[:, hs, :]), start=False, stop=False)
                    last = pe.matmul(o, upper[:, 1, :], flat(power[:, hs, :]), start=False, stop=True)
                last.then_inc(a_logits, 1)

            def unit(b, kt, g):
                u = units_to(b - 1) + 2 * kt + g
                if (kt, g) == (0, 0):
                    if b >= 2:
                        pe.wait_ge(mask_in[b % 2], 16 * (b // 2))
                    else:
                        pe.wait_ge(setup_dve, 3)
                    pe.wait_ge(qa_split, b + 1)
                    pe.wait_ge(a_ext, b + 1)
                    unit_logits(b, 0, 0)
                    if b:
                        pe.wait_ge(a_outsb, b)
                if (kt, g) != (b, 1):
                    unit_logits(b, kt + g, 1 - g)
                pe.wait_ge(a_prob, u + 1)
                pe.matmul(psum[0:65, 6 + g, :], vw[:, kt, 0:65], prob[:, u % 3, :],
                          start=(kt == 0), stop=(kt == b)).then_inc(a_used, 1)

            def turn_a(b):
                pe.wait_ge(a_outsb, b + 1)
                pe.wait_ge(b_pt, min(b + 2, NB))
                if b + 1 in INDEX_AT:
                    pe.wait_ge(relued, 2 * chunks_before(INDEX_AT[b + 1] + 1))
                for h in range(H):
                    last = pe.transpose(psum[:, 2 + h // 4, 65 * (h % 4):65 * (h % 4) + 65],
                                        out_a[:, h // 4, P * (h % 4):P * (h % 4) + P], ident[0:65, 0:65])
                last.then_inc(a_turned, 1)

            def columns(y, bank, done):
                for t in range(4):
                    last = pe.transpose(psum[:, bank, P * t:P * t + P],
                                        y[:, 2 * t:2 * t + 2, :].rearrange("p h d -> p (h d)"), ident[:, :])
                last.then_inc(done, 1)

            def columns_a(b):
                pe.wait_ge(a_y, b + 1)
                columns(y_a, 1, a_yt)

            def columns_b(b):
                pe.wait_ge(b_y, b + 1)
                columns(y_b, 0, b_yt)

            def index(p):
                b = {pair: at for at, pair in INDEX_AT.items()}[p]
                pe.wait_ge(b_gated, b + 1)
                pe.wait_ge(qi_lo_ok, p)

            run_steps({"index": index, "dots": lambda p, j, c, w: index_dots(p, j, c, w, 0), "turn_a": turn_a,
                       "columns_a": columns_a, "window": window_logits, "scan": max_logits, "turn_b": turn_b,
                       "minus_max": minus_max, "mix_b": mix_b, "columns_b": columns_b, "unit": unit})

            pe.wait_ge(a_gated, NB)
            pe.wait_ge(wo_lo_ok, KT)
            for b in range(NB):
                s = b % 2
                pe.wait_ge(yt_lo_ok, b + 1)
                if b >= 2:
                    pe.wait_ge(o_z, b - 1)
                for m in range(2):
                    cols = slice(512 * m, 512 * m + 512)
                    for k in range(KT):
                        for q, (yt, wt) in enumerate(((yt_hi, wo_hi), (yt_hi, wo_lo), (yt_lo, wo_hi))):
                            last = pe.matmul(psum[:, 2 * s + m, :], yt[:, s, k, :], wt[:, k, cols],
                                             start=(k == 0 and q == 0), stop=(k == KT - 1 and q == 2))
                last.then_inc(o_mm, 1)

        @block.vector
        def _(dve):
            v = nc.vector
            done = {"prep": 0, "trial": 0, "count": 0, "sum": 0, "b_step": 0}

            def step(ins):
                ins.then_inc(prep, 1)
                done["prep"] += 1
                dve.wait_ge(prep, done["prep"])

            def small(ins):
                ins.then_inc(b_step, 1)
                done["b_step"] += 1
                dve.wait_ge(b_step, done["b_step"])

            def index_begin(p):
                if p > 1:
                    dve.wait_ge(mask_out, 32 * (p - 1))

            def index_sum(p, j, c, w):
                n_chunk = chunks_before(p) + j * len(chunks(p)) + c // 512
                b = 2 * p + j
                dve.wait_ge(norm_out, b + 1)
                o = score[:, j, c:c + w]
                for h in range(IH):
                    if h % 2 == 0:
                        dve.wait_ge(relued, 2 * n_chunk + h // 2 + 1)
                    wt = vw[:, b, VN + 1 - IH + h:VN + 2 - IH + h]
                    if h == 0:
                        v.tensor_scalar(o, relu[:, h, 0:w], wt, 0.0, ALU.mult, ALU.add).then_inc(summed, 1)
                    else:
                        dve.wait_ge(summed, done["sum"])
                        v.scalar_tensor_tensor(o, relu[:, h, 0:w], wt, o, ALU.mult, ALU.add).then_inc(summed, 1)
                    done["sum"] += 1

            def sortable(p):
                n = nd(p)
                dve.wait_ge(summed, done["sum"])
                low = -3.0e38
                v.memset(score[0:HD, 0, n - P - HD:n - P], low)
                v.memset(score[0:HD, 1, n - HD:n], low)
                step(v.memset(score[:, 0, n - P:n], low))
                sc = score[:, :, 0:n].bitcast(I32)
                di = dist[:, :, 0:n].bitcast(I32)
                step(v.tensor_scalar(di, sc, 31, 0x7fffffff, ALU.arith_shift_right, ALU.bitwise_and))
                step(v.tensor_tensor(sc, sc, di, ALU.bitwise_xor))
                step(v.tensor_scalar(di, sc, -65536, None, ALU.bitwise_and))

            def search(p, eighth):
                n = nd(p)
                part = eighth // 4
                u = trial[:, part, :]
                if eighth == 0:
                    v.memset(u, -32768.0).then_inc(trial_ok, 1)
                    done["trial"] += 1
                if eighth == 4:
                    dve.wait_ge(trial_ok, done["trial"])
                    for j in range(2):
                        lows = score[:, j, 0:n].bitcast(U16).rearrange("p (n t) -> p n t", t=2)[:, :, 0]
                        last = v.scalar_tensor_tensor(dist[:, j, 0:n], dist[:, j, 0:n].bitcast(I32),
                                                      trial[:, 0, j:j + 1], lows, ALU.subtract, ALU.add)
                    step(last)
                    v.memset(u, 32767.5).then_inc(trial_ok, 1)
                    done["trial"] += 1
                for i in range(4):
                    dve.wait_ge(trial_ok, done["trial"])
                    src = dist[:, 0, 0:n].bitcast(I32) if part == 0 else dist[:, 0, 0:n]
                    v.tensor_scalar(above[:, 0, 0:n], src, u[:, 0:1], None, ALU.is_ge, ALU.add,
                                    accum_out=count[:, 0:1]).then_inc(counted, 1)
                    done["count"] += 1
                    dve.wait_ge(counted, done["count"])
                    v.tensor_scalar(accept[:, 0:1], count[:, 0:1], float(TOPK), 0.5, ALU.is_ge, ALU.subtract)
                    dve.wait_ge(signed, done["count"])
                    v.tensor_scalar(accept[:, 1:2], count[:, 1:2], float(n - 2 * TOPK), 0.5, ALU.is_le,
                                    ALU.subtract).then_inc(accepted, 1)
                    dve.wait_ge(accepted, done["count"])
                    step_size = steps[:, 4 * eighth + i:4 * eighth + i + 1]
                    v.scalar_tensor_tensor(u, accept[:, :], step_size, u, ALU.mult, ALU.add).then_inc(trial_ok, 1)
                    done["trial"] += 1

            def make_masks(p):
                n = nd(p)
                dve.wait_ge(trial_ok, done["trial"])
                for j in range(2):
                    t = trial[:, 1, j:j + 1]
                    v.tensor_scalar(above[:, j, 0:n], dist[:, j, 0:n], t, None, ALU.is_gt, ALU.add,
                                    accum_out=n_above[:, j:j + 1])
                    last = v.tensor_scalar(equal[:, j, 0:n], dist[:, j, 0:n], t, None, ALU.is_equal)
                step(last)
                for j in range(2):
                    last = v.tensor_tensor_scan(rank[:, j, 0:n], equal[:, j, 0:n], equal[:, j, 0:n],
                                                n_above[:, j:j + 1], ALU.add, ALU.max)
                step(last)
                step(v.scalar_tensor_tensor(equal[:, :, 0:n], rank[:, :, 0:n], float(TOPK), equal[:, :, 0:n],
                                            ALU.is_le, ALU.mult))
                step(v.scalar_tensor_tensor(above[:, :, 0:n], equal[:, :, 0:n], -1.0, above[:, :, 0:n],
                                            ALU.add, ALU.add))
                v.tensor_scalar(above[:, :, 0:n], above[:, :, 0:n], BIG, None, ALU.mult).then_inc(mask_ok, 1)

            dve.wait_ge(const_in, 32)
            def search_tiles(n, searching):
                if searching:
                    pair, per_tile = searching
                    for _ in range(n * per_tile):
                        eighth = done["count"] % 32 // 4
                        search(pair, eighth)
                        if eighth == 7:
                            make_masks(pair)

            for kind, *what in PLAN:
                if kind == "index":
                    p = what[0]
                    index_begin(p)
                    for j in range(2):
                        for c, w in chunks(p):
                            index_sum(p, j, c, w)
                    sortable(p)
                elif kind == "keys":
                    search_tiles(KEY_TILES, what[1])
                else:
                    search_tiles(what[2], what[4])

            for i in range(2):
                dve.wait_ge(stored[i], 16 * N_TILES)
            dve.wait_ge(setup_act, 1)
            v.memset(mask[:, 0, 0:P], 0.0)
            step(v.memset(mask[:, 1, 0:2 * P], 0.0))
            v.memset(mask[0:HD, 0, HD:P], -BIG)
            step(v.memset(mask[0:HD, 1, P + HD:2 * P], -BIG))
            v.tensor_scalar(ka_ext[96:98, 1, :], ka_ext[96:98, 1, :].bitcast(F32), -float(P), None,
                            ALU.add).then_inc(pos_ok, 1)
            v.memset(mb[:, :], 0.0).then_inc(setup_dve, 1)

            def window(b):
                j0 = HD if b == 0 else 0
                dve.wait_ge(b_logits, b + 1)
                if b:
                    dve.wait_ge(b_turned, b)
                ps = psum[:, 0:4, 0:2 * WIN].rearrange("p b (h j) -> p b h j", h=2)[:, :, :, j0:WIN]
                four = lambda t: t[:, :, :].rearrange("p (b h) j -> p b h j", h=2)[:, :, :, j0:WIN]
                v.tensor_tensor(four(lb), ps, four(bias), ALU.add).then_inc(b_biased, 1)
                dve.wait_ge(b_biased, b + 1)
                small(v.tensor_reduce(mb[:, :], lb[:, :, j0:WIN], AX_X, ALU.max))
                small(v.tensor_tensor(mb2[:, :], mb[:, :], sink8[:, :], ALU.max))
                small(v.tensor_scalar(nmb[:, :], mb2[:, :], -0.125, None, ALU.mult))
                v.tensor_tensor(zb[:, :], nmb[:, :], sink1[:, :], ALU.add).then_inc(b_max, 1)

            def scan_max(b, h):
                s = b % 2
                n_keys = P * (b + 1)
                if b >= 2 and h == 0:
                    dve.wait_ge(mask_in[s], 16 * (b // 2))
                scan = scans_to(b - 1) + h * (1 + (b >= 8))
                for ci, c in enumerate(range(0, n_keys, 1024)):
                    w = min(1024, n_keys - c)
                    dve.wait_ge(a_scan, scan + 1)
                    if scan >= 2:
                        dve.wait_ge(a_scanned, scan - 1)
                    src = psum[:, 2 * (scan % 2):2 * (scan % 2) + 2, :].rearrange("p b n -> p (b n)")[:, 0:w]
                    v.tensor_tensor_reduce(out=junk[:, scan % 2, 0:w], in0=src, in1=mask[:, s, c:c + w],
                                           scale=1.0, scalar=-3.0e38, op0=ALU.add, op1=ALU.max,
                                           accum_out=part_max[:, ci, h:h + 1]).then_inc(a_scanned, 1)
                    scan += 1
                if h < H - 1:
                    return
                dve.wait_ge(a_scanned, scan)
                if n_keys > 1024:
                    small(v.tensor_tensor(neg_max[:, :], part_max[:, 0, :], part_max[:, 1, :], ALU.max))
                    v.tensor_scalar(neg_max[:, :], neg_max[:, :], -1.0, None, ALU.mult).then_inc(a_neg, 1)
                else:
                    v.tensor_scalar(neg_max[:, :], part_max[:, 0, :], -1.0, None, ALU.mult).then_inc(a_neg, 1)

            def minus_max(b):
                s = b % 2
                dve.wait_ge(b_exp, b + 1)
                small(v.tensor_tensor(den_b[:, :], sum_b[:, :], ez[:, :], ALU.add))
                small(v.reciprocal(rec_b[:, :], den_b[:, :]))
                dve.wait_ge(a_negt, b + 1)
                v.tensor_tensor(qa_ext[HD:HD + H, s, :, :], psum[0:H, 1, 0:P].unsqueeze(1).broadcast_to([H, H, P]),
                                sel[:, :, :], ALU.mult).then_inc(a_ext, 1)

            def mix_b(b):
                dve.wait_ge(b_mixed, b + 1)
                if b:
                    dve.wait_ge(b_yt, b)
                v.tensor_tensor(y_b[:, :, :], psum[:, 0, :].rearrange("p (h d) -> p h d", h=H),
                                rec_b[:, :].unsqueeze(2).broadcast_to([P, H, HD]), ALU.mult).then_inc(b_y, 1)

            def gate_group(b, turned, bank, y, gate, gate_in, was_stored, gated):
                dve.wait_ge(turned, b + 1)
                dve.wait_ge(gate_in, 16 * (b + 1))
                if b:
                    dve.wait_ge(was_stored, 16 * b)
                v.tensor_tensor(flat(y[:, :, :]), psum[:, bank, :], flat(gate[:, :, :]), ALU.mult) \
                    .then_inc(gated, 1)

            def turn_a(b):
                dve.wait_ge(a_turned, b + 1)
                heads = [psum[:, 2 + g, 0:4 * 65].rearrange("p (h d) -> p h d", h=4) for g in range(2)]
                for g in range(2):
                    last = v.reciprocal(rec_a[:, 4 * g:4 * g + 4], heads[g][:, :, HD])
                last.then_inc(a_rec, 1)
                dve.wait_ge(a_rec, b + 1)
                for g in range(2):
                    last = v.tensor_tensor(y_a[:, 4 * g:4 * g + 4, :], heads[g][:, :, 0:HD],
                                           rec_a[:, 4 * g:4 * g + 4].unsqueeze(2).broadcast_to([P, 4, HD]),
                                           ALU.mult)
                last.then_inc(a_y, 1)
                if b + 2 < NB:
                    s = b % 2
                    v.tensor_scalar(ka_ext[96:98, s, :], ka_ext[96:98, s, :].bitcast(F32), -2.0 * P, None,
                                    ALU.add).then_inc(pos_ok, 1)

            run_steps({
                "index": index_begin, "dots": index_sum, "sortable": sortable, "search": search,
                "masks": make_masks, "turn_a": turn_a, "window": window, "scan": scan_max,
                "columns_a": lambda b: gate_group(b, a_yt, 1, yt_a, gate_a, gate_a_in, a_stored, a_gated),
                "minus_max": minus_max, "mix_b": mix_b,
                "columns_b": lambda b: gate_group(b, b_yt, 0, yt_b, gate_b, gate_b_in, b_stored, b_gated)})

            dve.wait_ge(ln_in, 32)
            n_o = 0
            for b in range(NB):
                s = b % 2
                r = z[:, b % 3, :]
                dve.wait_ge(o_mm, b + 1)
                dve.wait_ge(row_in[s], 32 * (b // 2 + 1))
                if b >= 3:
                    dve.wait_ge(out_dma[b % 3], 16 * (b // 3))
                v.scalar_tensor_tensor(r, x_row[:, s, :], ALPHA, psum[:, 2 * s:2 * s + 2, :]
                                       .rearrange("p b n -> p (b n)"), ALU.mult, ALU.add).then_inc(o_z, 1)
                dve.wait_ge(o_z, b + 1)
                for m in range(2):
                    last = v.bn_stats(stats[:, m, :], r[:, 512 * m:512 * m + 512])
                last.then_inc(o_step, 1)
                dve.wait_ge(o_step, n_o + 1)
                v.bn_aggr(moments[:, s, :], stats[:, :, :]).then_inc(o_step, 1)
                dve.wait_ge(o_step, n_o + 2)
                v.tensor_scalar(var_eps[:, s:s + 1], moments[:, s, 1:2], EPS, None, ALU.add).then_inc(o_var, 1)
                dve.wait_ge(o_rstd, b + 1)
                v.tensor_scalar(r, r, moments[:, s, 0:1], rstd[:, s:s + 1], ALU.subtract, ALU.mult) \
                    .then_inc(o_step, 1)
                dve.wait_ge(o_step, n_o + 3)
                v.tensor_tensor(r, r, gains[:, :], ALU.mult).then_inc(o_step, 1)
                dve.wait_ge(o_step, n_o + 4)
                v.tensor_tensor(r, r, shifts[:, :], ALU.add).then_inc(o_done, 1)
                n_o += 4


def round12(a):
    bits = a.view(np.uint32)
    odd = (bits >> np.uint32(12)) & np.uint32(1)
    return ((bits + np.uint32(0x7FF) + odd) & np.uint32(0xFFFFF000)).view(np.float32)


def shape_constants():
    slopes = np.array([2.0 ** (-8.0 * (i + 1) / (2 * H)) for i in range(2 * H)], np.float32)
    sa, sbl = slopes[0::2] * np.float32(8), slopes[1::2] * np.float32(8)
    sa_hi = round12(sa)
    sa_lo = sa - sa_hi
    eye = np.eye(P, dtype=np.float32)
    q = np.arange(P)
    upper = np.maximum(q[None, :] - q[:, None], 0).astype(np.float32)
    power = np.stack([-2.0 * 8 * 2.0 ** -h * eye for h in range(H)], 1).astype(np.float32)
    upper = upper * slopes[0]
    upper_hi = round12(upper)
    upper = np.stack([upper_hi, upper - upper_hi], 1)
    extm = np.zeros((P - HD, H, P), np.float32)
    extm[32] = sa_hi[:, None]
    extm[33] = sa_lo[:, None]
    extk = np.zeros((P - HD, L), np.float32)
    extk[0:H] = 1.0
    extk[32:34] = np.arange(L)
    j = np.arange(WIN)
    dist = np.abs(q[:, None] + HD - j[None, :]).astype(np.float32)
    seen = np.where(q[:, None] < HD, j[None, :] < P, j[None, :] >= HD)
    bias = np.where(seen[:, None, :], -sbl[None, :, None] * dist[:, None, :], np.float32(-BIG)).astype(np.float32)
    sel = np.repeat(np.eye(H, dtype=np.float32)[:, :, None], P, 2)
    steps = np.repeat(np.array([2.0 ** (31 - i) for i in range(32)], np.float32)[None], P, 0)
    return dict(c_step=steps, c_ident=eye, c_upper=upper, c_pow=power, c_extm=extm,
                c_extk=extk, c_bias=bias, c_sel=sel)

def kernel(**inputs):
    import concourse.bacc as bacc
    from concourse.bass_utils import run_bass_kernel_spmd

    nc = bacc.Bacc("TRN2", target_bir_lowering=False, num_devices=1)
    x = np.ascontiguousarray(inputs["x"])[0]
    w = np.ascontiguousarray(inputs["w_in"])[0]
    order = np.r_[1152:1408, 1408:1472, 512:576, 1988:2116, 0:512, 1476:1988, 640:1152, 2244:2756]
    w_tiles = w[:, order].reshape(KT, P, N_TILES, P).transpose(2, 1, 0, 3).reshape(N_TILES, P, KT * P)
    w_norm = w[:, np.r_[576:640, 2116:2244, 1472:1476]].reshape(KT, P, VN).transpose(1, 0, 2)
    w_out = np.asarray(inputs["w_out"])[0].reshape(KT, P, D).transpose(1, 0, 2)
    arrays = dict(xT=x.T, w_tiles=w_tiles, w_norm=w_norm, w_out=w_out, x_res=x,
                  sinks=np.asarray(inputs["sinks"]), ln_g=np.asarray(inputs["ln_g"]),
                  ln_b=np.asarray(inputs["ln_b"]), **shape_constants())
    arrays = {k: np.ascontiguousarray(a) for k, a in arrays.items()}
    args = {k: nc.dram_tensor(k, a.shape, F32, kind="ExternalInput").ap() for k, a in arrays.items()}
    args["proj"] = nc.dram_tensor("proj", (N_TILES * P, L), F32, kind="Internal").ap()
    args["masks"] = nc.dram_tensor("masks", (NB, P, L), BF16, kind="Internal").ap()
    args["y_t"] = nc.dram_tensor("y_t", (D, L), F32, kind="Internal").ap()
    args["out"] = nc.dram_tensor("out", (1, L, D), F32, kind="ExternalOutput").ap().rearrange("a l d -> (a l) d")
    hybrid_kernel(nc, **args)
    r = run_bass_kernel_spmd(nc, [arrays], core_ids=[0])
    return r.results[0]["out"]
```

```python
from contextlib import ExitStack

import numpy as np

import concourse.bass as bass
from concourse import mybir

F32 = mybir.dt.float32
F32R = mybir.dt.float32r
BF16 = mybir.dt.bfloat16
I32 = mybir.dt.int32
U16 = mybir.dt.uint16
I16 = mybir.dt.int16
ALU = mybir.AluOpType
ACT = mybir.ActivationFunctionType
AX_X = mybir.AxisListType.X

P = 128
L = 2048
D = 1024
KT = D // P
NB = L // P
NPAIR = NB // 2
HALF = L // 2
H = 8
HD = 64
IH = 4
TOPK = 256
BIG = float(2.0 ** 100)
N_TILES = 20
KEY_TILES = 4
VN = 196
WIN = 192
ROW_QI, ROW_KI, ROW_KA, ROW_KB, ROW_QA, ROW_QB, ROW_G = 0, 256, 320, 384, 512, 1024, 1536
ALPHA = 2.0 ** 0.25
EPS = 1e-5

PLAN = [("keys", 0), ("queries", 1), ("index", 1), ("queries", 2), ("tiles", 0, 4, 6, False, 1, (8, 8, 8, 8, 0, 0)),
        ("index", 2), ("queries", 3),
        ("tiles", 0, 10, 2, False, 2, (8, 8)), ("tiles", 0, 12, 4, True, 2, (8, 8, 0, 0)),
        ("index", 3), ("tiles", 0, 16, 4, True, 3, (5, 5, 5, 5)), ("keys", 1, 3, (4, 4, 4, 0)),
        ("queries", 4), ("index", 4), ("queries", 5), ("tiles", 1, 4, 8, False, 4, (5, 5, 5, 5, 5, 5, 2, 0)),
        ("index", 5), ("tiles", 1, 12, 8, True, 5, (4, 4, 4, 4, 4, 4, 4, 4))]
SEARCH_AT = {1: (6, 0, 5), 2: (6, 5, 5), 3: (6, 10, 5), 4: (6, 15, 5), 5: (6, 20, 6), 6: (6, 26, 6),
             8: (7, 0, 6), 9: (7, 6, 6), 10: (7, 12, 5), 11: (7, 17, 5), 12: (7, 22, 5), 13: (7, 27, 5)}
INDEX_AT = {0: 6, 7: 7}
MASKS_AT = {b: pair for b, (pair, first, n) in SEARCH_AT.items() if first + n == 32}

WAIT = {"count": 0.072, "turn_a": 1.8, "columns_a": 0.405, "window": 4.6, "scan": 1.875,
        "exp_b": 0.3, "turn_b": 2.34, "mix_b": 0.23, "columns_b": 0.64, "masks": 20,
        "index": 1.54, "dots": 3.3, "sortable": 20.0}


def attention_step(b):
    pieces = []
    pair, first, n = SEARCH_AT.get(b, (0, 0, 0))
    begun = 0

    def search_step(last=False):
        nonlocal begun
        if begun and begun <= n:
            pieces.append((("decide", pair, first + begun - 1), 0.3))
        if begun < n and not last:
            pieces.append((("count", pair, first + begun), WAIT["count"] * (pair + 1)))
        begun += 1

    if b >= 2:
        pieces += [(("turn_a", b - 2), WAIT["turn_a"]), (("columns_a", b - 2), WAIT["columns_a"])]
    if b < NB:
        pieces.append((("window", b), WAIT["window"]))
        scans = [(h, c) for h in range(H) for c in range(0, P * (b + 1), 1024)]
        every = len(scans) // H
        pieces += [(("max_logits", b, *scans[0]), 0.0), (("max_logits", b, *scans[1]), 0.0)]
        for k, scan in enumerate(scans):
            pieces.append((("scan", b, *scan), WAIT["scan"] * min(1.0, P * (b + 1) / 1024 - scan[1] / 1024)))
            if k % every == every - 1:
                search_step()
                if k // every >= 2:
                    pieces.append((("exp_b", b, k // every - 2), 0.0))
            if k + 2 < len(scans):
                pieces.append((("max_logits", b, *scans[k + 2]), 0.0))
        search_step(last=True)
        if b in INDEX_AT:
            pieces.append((("queries", INDEX_AT[b]), 0.0))
        if b in MASKS_AT:
            pieces.append((("masks", MASKS_AT[b]), WAIT["masks"]))
        pieces += [(("exp_b", b, H - 2), 0.0), (("exp_b", b, H - 1), WAIT["exp_b"]), (("turn_b", b), WAIT["turn_b"])]
        pieces.append((("minus_max", b), 0.0))
        pieces.append((("mix_b", b), WAIT["mix_b"]))
        if b + 1 < NB:
            pieces.append((("next_b", b + 1), 0.0))
        pieces.append((("columns_b", b), WAIT["columns_b"]))
    if b in INDEX_AT:
        pair = INDEX_AT[b]
        pieces += [(("index", pair), WAIT["index"])]
        n = 2 * P * (pair + 1)
        for j in range(2):
            for c in range(0, n, 512):
                pieces.append((("dots", pair, j, c, min(512, n - c)), WAIT["dots"]))
        pieces.append((("sortable", pair), WAIT["sortable"]))
    units = [("unit", b - 1, kt, g) for kt in range(b) for g in range(2)] if 1 <= b <= NB else []
    total, so_far, placed, order = sum(w for _, w in pieces), 0.0, 0, []
    for piece, weight in pieces:
        order.append(piece)
        so_far += weight
        upto = round(len(units) * so_far / total)
        order += units[placed:upto]
        placed = max(placed, upto)
    order += units[placed:]
    if units:
        order.append(("leave_a", b - 1))
    if b + 1 < NB:
        order.append(("next_a", b + 1))
    if b >= NB - 1:
        work = [("w_out", k) for k in range(4 * (b - NB + 1), 4 * (b - NB + 2))] if b <= NB else []
        work += [("split_y", 0), ("split_y", 1)] if b == NB else []
        places = [i for i, piece in enumerate(order) if piece[0] == "unit"]
        for n in reversed(range(len(work))):
            order.insert(places[len(places) * (n + 1) // (len(work) + 1)] + 1, work[n])
    if b == NB + 1:
        order.insert(0, ("project", 0))
    return order


def run_steps(engine_pieces):
    for b in range(NB + 2):
        for kind, *what in attention_step(b):
            if kind in engine_pieces:
                engine_pieces[kind](*what)


def hybrid_kernel(nc, xT, w_tiles, w_norm, w_out, x_res, sinks, ln_g, ln_b, c_step, c_ident,
                  c_upper, c_pow, c_extm, c_extk, c_bias, c_sel, proj, masks, y_t, out):
    with ExitStack() as ctx:
        def sem(name):
            return ctx.enter_context(nc.semaphore(name))

        def sb(stack, name, shape, dt):
            return stack.enter_context(nc.sbuf_tensor(name, shape, dt))

        psum = ctx.enter_context(nc.psum_tensor("psum", [P, 8, 512], F32))

        vw = sb(ctx, "vw", [P, NB, 200], F32)
        ident = sb(ctx, "ident", [P, P], F32)
        steps = sb(ctx, "steps", [P, 32], F32)
        trial = sb(ctx, "trial", [P, 2, 2], F32)
        count = sb(ctx, "count", [P, 2], F32)
        accept = sb(ctx, "accept", [P, 2], F32)
        n_above = sb(ctx, "n_above", [P, 2], F32)
        with ExitStack() as topk:
            ki_hi = sb(topk, "ki_hi", [P, L], F32R)
            ki_lo = sb(topk, "ki_lo", [HD, L], F32R)
            qi_raw = sb(topk, "qi_raw", [P, IH, 2 * P], F32)
            qi_split = sb(topk, "qi_split", [P, IH, 2 * P], F32R)
            relu = sb(topk, "relu", [P, IH, 512], F32)
            score = sb(topk, "score", [P, 2, L], F32)
            dist = sb(topk, "dist", [P, 2, L], F32)
            above = sb(topk, "above", [P, 2, L], BF16)
            half_rows = score[:, :, :].bitcast(BF16)
            equal = half_rows[:, :, 0:L]
            rank = score[:, :, :].bitcast(I16)[:, :, L:2 * L]
            with ExitStack() as early:
                x_hi = sb(early, "x_hi", [P, KT, HALF], F32R)
                x_lo = sb(early, "x_lo", [P, KT, HALF], F32R)
                raw = sb(early, "raw", [P, 2, KT * P], F32)
                w_hi = sb(early, "w_hi", [P, 2, KT, P], F32R)
                w_lo = sb(early, "w_lo", [P, 2, KT, P], F32R)
                wn_hi = sb(early, "wn_hi", [P, KT, VN], F32R)
                wn_lo = sb(early, "wn_lo", [P, KT, VN], F32R)
                staged = sb(early, "staged", [P, 2, HALF], F32)
                ki_raw = sb(early, "ki_raw", [P, HALF], F32)
            with ExitStack() as late:
                qb_raw = sb(late, "qb_raw", [P, H, P], F32)
                kb_raw = sb(late, "kb_raw", [P, 2, WIN], F32)
                qb_mix = sb(late, "qb_mix", [P, H, P], F32R)
                kb_hi = sb(late, "kb_hi", [P, 2, WIN], F32R)
                kb_lo = sb(late, "kb_lo", [HD, 2, WIN], F32R)
                bias = sb(late, "bias", [P, H, WIN], F32)
                lb = sb(late, "lb", [P, H, WIN], F32)
                ptb_own = sb(late, "ptb_own", [P, H, P], F32)
                ptb_prev = sb(late, "ptb_prev", [P, H, P], F32)
                ka_ext = sb(late, "ka_ext", [P, 2, L], F32R)
                ka_mix = sb(late, "ka_mix", [P, L], F32R)
                qa_raw = sb(late, "qa_raw", [P, H, P], F32)
                gate_a = sb(late, "gate_a", [P, 4, P], F32)
                gate_b = sb(late, "gate_b", [P, 4, P], F32)
                mask = sb(late, "mask", [P, 2, L], BF16)
                qa_ext = sb(late, "qa_ext", [P, 2, H, P], F32R)
                qa_mix = sb(late, "qa_mix", [P, 2, H, P], F32R)
                upper = sb(late, "upper", [P, 2, P], F32R)
                power = sb(late, "power", [P, H, P], F32R)
                ident4 = sb(late, "ident4", [P, 4, P], BF16)
                sel = sb(late, "sel", [H, H, P], BF16)
                prob = sb(late, "prob", [P, 3, 512], F32)
                out_a = sb(late, "out_a", [65, 2, 512], F32)
                y_a = sb(late, "y_a", [P, H, HD], F32)
                y_b = sb(late, "y_b", [P, H, HD], F32)
                yt_a = sb(late, "yt_a", [P, 4, P], F32)
                yt_b = sb(late, "yt_b", [P, 4, P], F32)
                junk = sb(late, "junk", [P, 2, 1024], BF16)
                part_max = sb(late, "part_max", [P, 2, H], F32)
                neg_max = sb(late, "neg_max", [P, H], F32)
                sink8 = sb(late, "sink8", [P, H], F32)
                sink1 = sb(late, "sink1", [P, H], F32)
                mb = sb(late, "mb", [P, H], F32)
                mb2 = sb(late, "mb2", [P, H], F32)
                nmb = sb(late, "nmb", [P, H], F32)
                zb = sb(late, "zb", [P, H], F32)
                ez = sb(late, "ez", [P, H], F32)
                sum_b = sb(late, "sum_b", [P, H], F32)
                den_b = sb(late, "den_b", [P, H], F32)
                rec_b = sb(late, "rec_b", [P, H], F32)
                rec_a = sb(late, "rec_a", [P, H], F32)
        with ExitStack() as last:
            wo_raw = sb(last, "wo_raw", [P, 2, D], F32)
            wo_hi = sb(last, "wo_hi", [P, KT, D], F32R)
            wo_lo = sb(last, "wo_lo", [P, KT, D], F32R)
            yt_raw = sb(last, "yt_raw", [P, 2, KT, P], F32)
            yt_hi = sb(last, "yt_hi", [P, 2, KT, P], F32R)
            yt_lo = sb(last, "yt_lo", [P, 2, KT, P], F32R)
            x_row = sb(last, "x_row", [P, 2, D], F32)
            z = sb(last, "z", [P, 3, D], F32)
            gains = sb(last, "gains", [P, D], F32)
            shifts = sb(last, "shifts", [P, D], F32)
            stats = sb(last, "stats", [P, 2, 6], F32)
            moments = sb(last, "moments", [P, 2, 2], F32)
            var_eps = sb(last, "var_eps", [P, 2], F32)
            minus_half = sb(last, "minus_half", [P, 1], F32)
            rstd = sb(last, "rstd", [P, 2], F32)

        raw_in = [sem(f"raw_in{i}") for i in range(2)]
        hi_done = sem("hi_done")
        lo_done = sem("lo_done")
        x_used = sem("x_used")
        tile_mm = sem("tile_mm")
        tile_out = sem("tile_out")
        stored = [sem(f"stored{i}") for i in range(2)]
        norm_mm = sem("norm_mm")
        norm_out = sem("norm_out")
        const_in = sem("const_in")
        ki_in = sem("ki_in")
        ki_hi_ok = sem("ki_hi_ok")
        ki_lo_ok = sem("ki_lo_ok")
        qi_in = sem("qi_in")
        qi_hi_ok = sem("qi_hi_ok")
        qi_lo_ok = sem("qi_lo_ok")
        dots = sem("dots")
        relued = sem("relued")
        summed = sem("summed")
        trial_ok = sem("trial_ok")
        counted = sem("counted")
        signed = sem("signed")
        accepted = sem("accepted")
        prep = sem("prep")
        mask_ok = sem("mask_ok")
        mask_out = sem("mask_out")
        stage_in = [sem(f"stage_in{i}") for i in range(3)]
        keys_taken = sem("keys_taken")
        late_in = sem("late_in")
        bias_in = sem("bias_in")
        sink_in = sem("sink_in")
        setup_act = sem("setup_act")
        setup_pool = sem("setup_pool")
        setup_dve = sem("setup_dve")
        qa_in = sem("qa_in")
        qb_in = sem("qb_in")
        gate_a_in = sem("gate_a_in")
        gate_b_in = sem("gate_b_in")
        mask_in = [sem(f"mask_in{i}") for i in range(2)]
        qa_round = sem("qa_round")
        qb_round = sem("qb_round")
        qa_zero = sem("qa_zero")
        qa_split = sem("qa_split")
        qb_split = sem("qb_split")
        pos_ok = sem("pos_ok")
        b_logits = sem("b_logits")
        b_biased = sem("b_biased")
        b_step = sem("b_step")
        b_max = sem("b_max")
        b_exp = sem("b_exp")
        b_turned = sem("b_turned")
        b_pt = sem("b_pt")
        b_mixed = sem("b_mixed")
        b_y = sem("b_y")
        b_yt = sem("b_yt")
        b_gated = sem("b_gated")
        b_stored = sem("b_stored")
        a_scan = sem("a_scan")
        a_scanned = sem("a_scanned")
        a_neg = sem("a_neg")
        a_negt = sem("a_negt")
        a_ext = sem("a_ext")
        a_logits = sem("a_logits")
        a_prob = sem("a_prob")
        a_used = sem("a_used")
        a_outsb = sem("a_outsb")
        a_turned = sem("a_turned")
        a_rec = sem("a_rec")
        a_y = sem("a_y")
        a_yt = sem("a_yt")
        a_gated = sem("a_gated")
        a_stored = sem("a_stored")
        wo_in = [sem(f"wo_in{i}") for i in range(2)]
        wo_hi_ok = sem("wo_hi_ok")
        wo_lo_ok = sem("wo_lo_ok")
        row_in = [sem(f"row_in{i}") for i in range(2)]
        y_in = [sem(f"y_in{i}") for i in range(2)]
        yt_hi_ok = sem("yt_hi_ok")
        yt_lo_ok = sem("yt_lo_ok")
        o_mm = sem("o_mm")
        o_z = sem("o_z")
        o_step = sem("o_step")
        o_var = sem("o_var")
        o_rstd = sem("o_rstd")
        o_done = sem("o_done")
        out_dma = [sem(f"out_dma{i}") for i in range(3)]
        ln_in = sem("ln_in")

        HALF_ITEM = [0, N_TILES + KT + 2]

        def item_of(half, tile):
            return HALF_ITEM[half] + tile + (KT if tile >= 1 else 0) + (2 if half == 0 and tile >= 2 else 0)

        def tile_ahead(half, first, n):
            return first + 2, min(n, N_TILES - 2 - first)

        def units_to(b):
            return (b + 1) * (b + 2)

        def scans_to(b):
            return H * sum(1 + (i >= 8) for i in range(b + 1))

        def nd(p):
            return 2 * P * (p + 1)

        def chunks(p):
            return [(c, min(512, nd(p) - c)) for c in range(0, nd(p), 512)]

        def chunks_before(p):
            return sum(2 * len(chunks(i)) for i in range(1, p))

        def tile_pairs(engine, g0, n, body):
            if g0 == 0 or n <= 2:
                for i in range(n // 2):
                    body(i)
            else:
                with engine.Fori(0, n // 2) as i:
                    body(i)

        def wait_if(engine, s, value):
            if not (isinstance(value, int) and value <= 0):
                engine.wait_ge(s, value)

        def proj_tile(tile, half):
            return proj.rearrange("(t p) n -> t p n", p=P)[bass.ds(tile, 1), :, half * HALF:(half + 1) * HALF] \
                .rearrange("a p n -> p (a n)")

        def flat(t):
            return t.rearrange("p h q -> p (h q)")

        x_view = xT.rearrange("(k p) t -> k p t", p=P)
        block = ctx.enter_context(nc.Block())

        @block.sync
        def _(sp):
            sp.dma_start(ident[:, :], c_ident).then_inc(const_in, 16)
            sp.dma_start(steps[:, :], c_step).then_inc(const_in, 16)

            def load_tiles(half, first, n):
                first, n = tile_ahead(half, first, n)
                base = item_of(half, first)

                def body(i):
                    for u in range(2):
                        sp.wait_ge(lo_done, i * 2 + (base + u - 1))
                        sp.dma_start(raw[:, u, :], w_tiles[bass.ds(i * 2 + (first + u), 1), :, :]
                                     .rearrange("a p n -> p (a n)")).then_inc(raw_in[u], 16)

                tile_pairs(sp, first, n, body)

            def load_item(n, src, width):
                if n >= 2:
                    sp.wait_ge(lo_done, n - 1)
                sp.dma_start(raw[:, n % 2, 0:width], src).then_inc(raw_in[n % 2], 16)

            def load_index(p):
                for i in range(2):
                    sp.wait_ge(stored[i], 16 * (p // 4 * N_TILES // 2 + 1))
                if p > 1:
                    sp.wait_ge(qi_lo_ok, p - 1)
                for r in range(2):
                    sp.dma_start(qi_raw[HD * r:HD * r + HD, :, :],
                                 proj[ROW_QI:ROW_QI + IH * HD, 2 * P * p:2 * P * p + 2 * P]
                                 .rearrange("(h d) t -> d h t", d=HD)).then_inc(qi_in, 16)

            def load_keys(half):
                load_item(item_of(half, 0), w_tiles[0], KT * P)
                for k in range(KT):
                    load_item(item_of(half, 0) + 1 + k, x_view[k, :, half * HALF:(half + 1) * HALF], HALF)
                load_item(item_of(half, 1), w_tiles[1], KT * P)
                if half == 0:
                    for j in range(2):
                        load_item(item_of(0, 1) + 1 + j,
                                  w_norm[:, 4 * j:4 * j + 4, :].rearrange("p k n -> p (k n)"), 4 * VN)
                load_tiles(half, 0, KEY_TILES)

            for kind, *what in PLAN:
                if kind == "keys":
                    load_keys(what[0])
                elif kind == "queries":
                    load_index(what[0])
                elif kind == "tiles":
                    load_tiles(*what[:3])

            for i in range(2):
                sp.wait_ge(stored[i], 16 * N_TILES)
            sp.wait_ge(ki_lo_ok, 2)
            for i, stage in enumerate((qa_raw, qb_raw)):
                for r in range(2):
                    sp.dma_start(flat(stage[HD * r:HD * r + HD, :, :]),
                                 proj[ROW_KA:ROW_KA + HD, HALF * i:HALF * (i + 1)]).then_inc(stage_in[i], 16)
            sp.dma_start(gate_a[0:H, :, :], c_sel[:, 0:4, :]).then_inc(stage_in[2], 16)
            sp.dma_start(gate_b[0:H, :, :], c_sel[:, 4:8, :]).then_inc(stage_in[2], 16)
            sp.dma_start(sink1[:, :], sinks.broadcast_to([P, H])).then_inc(sink_in, 16)
            sp.dma_start(bias[:, :, :], c_bias).then_inc(bias_in, 16)
            sp.wait_ge(keys_taken, 2)
            sp.wait_ge(setup_pool, 3)

            def load_qa(b):
                if b:
                    sp.wait_ge(qa_split, b)
                for r in range(2):
                    sp.dma_start(qa_raw[HD * r:HD * r + HD, :, :], proj[ROW_QA:ROW_QA + H * HD, P * b:P * b + P]
                                 .rearrange("(h d) t -> d h t", d=HD)).then_inc(qa_in, 16)

            def load_qb(b):
                if b:
                    sp.wait_ge(qb_split, b)
                j0 = HD if b == 0 else 0
                for r in range(2):
                    rows = slice(HD * r, HD * r + HD)
                    sp.dma_start(qb_raw[rows, :, :], proj[ROW_QB:ROW_QB + H * HD, P * b:P * b + P]
                                 .rearrange("(h d) t -> d h t", d=HD)).then_inc(qb_in, 16)
                    sp.dma_start(kb_raw[rows, :, j0:WIN], proj[ROW_KB:ROW_KB + P, P * b - HD + j0:P * b + P]
                                 .rearrange("(g d) t -> d g t", d=HD)).then_inc(qb_in, 16)

            def load_gate(t, row, b, s):
                sp.dma_start(t[:, :, :], proj[row:row + 4 * P, P * b:P * b + P]
                             .rearrange("(t p) n -> p t n", p=P)).then_inc(s, 16)

            def store_masks(p):
                sp.wait_ge(mask_ok, p)
                for j in range(2):
                    sp.dma_start(masks[2 * p + j, :, 0:nd(p)], above[:, j, 0:nd(p)]).then_inc(mask_out, 16)

            def load_rows(b):
                s = b % 2
                if b >= 2:
                    sp.wait_ge(yt_lo_ok, b - 1)
                sp.dma_start(yt_raw[:, s, :, :], y_t[:, P * b:P * b + P]
                             .rearrange("(k p) t -> p k t", p=P)).then_inc(y_in[s], 16)
                if b >= 2:
                    sp.wait_ge(o_z, b - 1)
                sp.dma_start(x_row[:, s, :], x_res[P * b:P * b + P, :]).then_inc(row_in[s], 16)

            load_qb(0)
            load_qa(0)
            sp.wait_ge(setup_act, 1)
            load_gate(gate_b, ROW_G + 4 * P, 0, gate_b_in)
            store_masks(5)
            for b in range(NB + 2):
                if 2 <= b < NB:
                    sp.wait_ge(mask_out, 32 * (b // 2))
                    sp.wait_ge(a_used, units_to(b - 2))
                    sp.dma_start(mask[:, b % 2, 0:P * (b + 1)], masks[b, :, 0:P * (b + 1)]) \
                        .then_inc(mask_in[b % 2], 16)
                if b in INDEX_AT:
                    load_index(INDEX_AT[b])
                if b + 1 < NB:
                    load_qb(b + 1)
                    load_qa(b + 1)
                if b in (NB - 1, NB):
                    sp.wait_ge(mask_out, 32 * (NPAIR - 1))
                    for k in range(4 * (b - NB + 1), 4 * (b - NB + 2)):
                        if k >= 2:
                            sp.wait_ge(wo_lo_ok, k - 1)
                        sp.dma_start(wo_raw[:, k % 2, :], w_out[:, k, :]).then_inc(wo_in[k % 2], 16)
                if b == NB:
                    sp.wait_ge(b_gated, NB)
                    sp.wait_ge(a_stored, 16 * 2)
                    load_rows(0)
                    load_rows(1)
                if 0 < b < NB:
                    sp.wait_ge(b_gated, b)
                    load_gate(gate_b, ROW_G + 4 * P, b, gate_b_in)
                if 1 <= b <= NB:
                    if b >= 2:
                        sp.wait_ge(a_gated, b - 1)
                    load_gate(gate_a, ROW_G, b - 1, gate_a_in)
                if b in MASKS_AT:
                    store_masks(MASKS_AT[b])

            sp.wait_ge(a_gated, NB)
            sp.wait_ge(a_stored, 16 * NB)
            sp.wait_ge(b_stored, 16 * NB)
            sp.dma_start(gains[:, :], ln_g.broadcast_to([P, D])).then_inc(ln_in, 16)
            sp.dma_start(shifts[:, :], ln_b.broadcast_to([P, D])).then_inc(ln_in, 16)
            for b in range(2, NB):
                load_rows(b)
            for i in range(3):
                sp.wait_ge(out_dma[i], 16 * len(range(i, NB, 3)))

        @block.gpsimd
        def _(pool):
            nc.gpsimd.memset(vw[:, :, 64:65], 1.0).then_inc(setup_pool, 1)

            def split_tile(n, u):
                pool.wait_ge(hi_done, n + 1)
                nc.gpsimd.tensor_tensor(w_lo[:, u, :, :].rearrange("p k c -> p (k c)"), raw[:, u, :],
                                        w_hi[:, u, :, :].bitcast(F32).rearrange("p k c -> p (k c)"),
                                        ALU.subtract).then_inc(lo_done, 1)

            def split_tiles(half, first, n):
                first, n = tile_ahead(half, first, n)
                base = item_of(half, first)

                def body(i):
                    for u in range(2):
                        split_tile(i * 2 + (base + u), u)

                tile_pairs(pool, first, n, body)

            def split_index(p, items):
                pool.wait_ge(lo_done, items)
                pool.wait_ge(qi_hi_ok, p)
                nc.gpsimd.tensor_tensor(qi_split[HD:P, :, :], qi_raw[HD:P, :, :],
                                        qi_split[HD:P, :, :].bitcast(F32), ALU.subtract).then_inc(qi_lo_ok, 1)
                pool.wait_ge(qi_lo_ok, p)

            def split_keys(half):
                split_tile(item_of(half, 0), 0)
                for k in range(KT):
                    n = item_of(half, 0) + 1 + k
                    pool.wait_ge(hi_done, n + 1)
                    nc.gpsimd.tensor_tensor(x_lo[:, k, :], raw[:, n % 2, :], x_hi[:, k, :].bitcast(F32),
                                            ALU.subtract).then_inc(lo_done, 1)
                split_tile(item_of(half, 1), 1)
                if half == 0:
                    for j in range(2):
                        n = item_of(0, 1) + 1 + j
                        pool.wait_ge(hi_done, n + 1)
                        nc.gpsimd.tensor_tensor(
                            wn_lo[:, 4 * j:4 * j + 4, :].rearrange("p k n -> p (k n)"), raw[:, n % 2, 0:4 * VN],
                            wn_hi[:, 4 * j:4 * j + 4, :].bitcast(F32).rearrange("p k n -> p (k n)"),
                            ALU.subtract).then_inc(lo_done, 1)
                split_tiles(half, 0, KEY_TILES)
                pool.wait_ge(ki_hi_ok, half + 1)
                nc.gpsimd.tensor_tensor(ki_lo[:, half * HALF:(half + 1) * HALF], ki_raw[0:HD, :],
                                        ki_hi[0:HD, half * HALF:(half + 1) * HALF].bitcast(F32),
                                        ALU.subtract).then_inc(ki_lo_ok, 1)

            items = 0
            for kind, *what in PLAN:
                if kind == "keys":
                    split_keys(what[0])
                    items = item_of(what[0], KEY_TILES + 2)
                elif kind == "queries":
                    split_index(what[0], items)
                elif kind == "tiles":
                    split_tiles(*what[:3])
                    items = item_of(what[0], min(what[1] + what[2] + 2, N_TILES))

            for i in range(2):
                pool.wait_ge(stored[i], 16 * N_TILES)
            pool.wait_ge(ki_lo_ok, 2)
            for i in range(2):
                pool.dma_start(ka_ext[HD:P, i, :], c_extk.bitcast(F32R)).then_inc(late_in, 16)
                pool.dma_start(qa_ext[HD:P, i, :, :], c_extm.bitcast(F32R)).then_inc(late_in, 16)
            pool.dma_start(power[:, :, :], c_pow.bitcast(F32R)).then_inc(late_in, 16)
            pool.dma_start(upper[:, :, :], c_upper.bitcast(F32R)).then_inc(late_in, 16)
            for i, stage in enumerate((qa_raw, qb_raw)):
                pool.wait_ge(setup_dve, 1 + i)
                nc.gpsimd.tensor_tensor(ka_mix[0:HD, HALF * i:HALF * (i + 1)], flat(stage[0:HD, :, :]),
                                        ka_ext[0:HD, 0, HALF * i:HALF * (i + 1)].bitcast(F32),
                                        ALU.subtract).then_inc(setup_pool, 1)
            pool.wait_ge(setup_pool, 3)
            nc.gpsimd.memset(neg_max[:, :], 0.0).then_inc(setup_pool, 1)
            pool.wait_ge(setup_pool, 4)

            def split_qb(b):
                j0 = HD if b == 0 else 0
                pool.wait_ge(qb_round, b + 1)
                nc.gpsimd.tensor_tensor(kb_lo[:, :, j0:WIN], kb_raw[0:HD, :, j0:WIN],
                                        kb_hi[0:HD, :, j0:WIN].bitcast(F32), ALU.subtract)
                nc.gpsimd.tensor_tensor(qb_mix[HD:P, :, :], qb_raw[HD:P, :, :],
                                        qb_mix[HD:P, :, :].bitcast(F32), ALU.subtract).then_inc(qb_split, 1)

            def split_qa(b):
                s = b % 2
                if b >= 2:
                    pool.wait_ge(a_used, units_to(b - 2))
                else:
                    pool.wait_ge(setup_act, 1)
                    pool.wait_ge(late_in, 16 * 6)
                nc.gpsimd.memset(qa_ext[HD:HD + H, s, :, :].bitcast(F32), 0.0).then_inc(qa_zero, 1)
                pool.wait_ge(qa_round, b + 1)
                nc.gpsimd.tensor_tensor(qa_mix[HD:P, s, :, :], qa_raw[HD:P, :, :],
                                        qa_mix[HD:P, s, :, :].bitcast(F32), ALU.subtract).then_inc(qa_split, 1)

            def store_a(b):
                pool.wait_ge(a_gated, b + 1)
                pool.dma_start(y_t[0:4 * P, P * b:P * b + P].rearrange("(k p) t -> p k t", p=P),
                               yt_a[:, :, :]).then_inc(a_stored, 16)

            def store_b(b):
                pool.wait_ge(b_gated, b + 1)
                pool.dma_start(y_t[4 * P:D, P * b:P * b + P].rearrange("(k p) t -> p k t", p=P),
                               yt_b[:, :, :]).then_inc(b_stored, 16)

            def split_w_out(k):
                if k == 0:
                    pool.wait_ge(qa_split, NB)
                pool.wait_ge(wo_hi_ok, k + 1)
                nc.gpsimd.tensor_tensor(wo_lo[:, k, :], wo_raw[:, k % 2, :], wo_hi[:, k, :].bitcast(F32),
                                        ALU.subtract).then_inc(wo_lo_ok, 1)
            def split_y(b):
                s = b % 2
                pool.wait_ge(yt_hi_ok, b + 1)
                nc.gpsimd.tensor_tensor(yt_lo[:, s, :, :], yt_raw[:, s, :, :],
                                        yt_hi[:, s, :, :].bitcast(F32), ALU.subtract).then_inc(yt_lo_ok, 1)

            split_qb(0)
            split_qa(0)
            run_steps({"queries": lambda p: split_index(p, items), "columns_a": store_a, "columns_b": store_b,
                       "next_b": split_qb, "next_a": split_qa, "w_out": split_w_out,
                       "split_y": split_y})
            pool.wait_ge(a_gated, NB)
            nc.gpsimd.memset(minus_half[:, :], -0.5).then_inc(setup_pool, 1)
            pool.wait_ge(setup_pool, 5)
            for b in range(NB + 1):
                if 2 <= b < NB:
                    split_y(b)
                if b:
                    s = (b - 1) % 2
                    pool.wait_ge(o_var, b)
                    nc.gpsimd.tensor_tensor(rstd[:, s:s + 1], var_eps[:, s:s + 1], minus_half[:, :],
                                            ALU.pow).then_inc(o_rstd, 1)

        @block.scalar
        def _(act):
            done = {"count": 0}

            def copy(dst, src, **kw):
                return nc.scalar.activation(dst, src, ACT.Copy, **kw)

            def round_item(n, dst, src):
                act.wait_ge(raw_in[n % 2], 16 * (n // 2 + 1))
                copy(dst, src).then_inc(hi_done, 1)

            def round_tile(n, u):
                act.wait_ge(raw_in[u], n)
                nc.scalar.activation(w_hi[:, u, :, :].rearrange("p k c -> p (k c)"), raw[:, u, :],
                                     ACT.Copy).then_inc(hi_done, 1)

            def evacuate(g, u, gated):
                act.wait_ge(tile_mm, g + 1)
                wait_if(act, stored[u], 16 * (g // 2) if isinstance(g, int) else (g - u) * 8)
                nc.scalar.activation(staged[:, u, :], psum[:, 2 * u:2 * u + 2, :].rearrange("p b n -> p (b n)"),
                                     ACT.Silu if gated else ACT.Copy).then_inc(tile_out, 1)

            def store(g, tile, half, u):
                act.wait_ge(tile_out, g + 1)
                act.dma_start(proj_tile(tile, half), staged[:, u, :]).then_inc(stored[u], 16)

            def tiles(half, first, n, gated, pair=None, per_tile=()):
                for t in range(first, first + n):
                    g, u = half * N_TILES + t, t % 2
                    evacuate(g, u, gated)
                    if t + 2 < N_TILES:
                        round_tile(16 * (item_of(half, t + 2) // 2 + 1), u)
                    elif (half, t) == (0, N_TILES - 2):
                        begin_half(1)
                    elif (half, t) == (0, N_TILES - 1):
                        round_tile(16 * (item_of(1, 1) // 2 + 1), 1)
                    store(g, t, half, u)
                    if pair:
                        for _ in range(per_tile[t - first]):
                            count_step(pair, done["count"] % 32)

            def store_masks(p):
                act.wait_ge(mask_ok, p)
                for j in range(2):
                    act.dma_start(masks[2 * p + j, :, 0:nd(p)], above[:, j, 0:nd(p)]).then_inc(mask_out, 16)

            def count_step(p, i):
                n = nd(p)
                part = i // 16
                src = dist[:, 1, 0:n].bitcast(I32) if part == 0 else dist[:, 1, 0:n]
                act.wait_ge(trial_ok, done["count"] + 2 * (p - 1) + 1 + part)
                nc.scalar.activation(above[:, 1, 0:n], src, ACT.Sign, scale=-1.0, bias=trial[:, part, 1:2],
                                     accum_out=count[:, 1:2]).then_inc(signed, 1)
                done["count"] += 1

            def begin_half(half):
                round_tile(16 * (item_of(half, 0) // 2 + 1), 0)
                for k in range(KT):
                    if half == 1:
                        act.wait_ge(*((x_used, k + 1) if k < KT - 1 else (tile_mm, N_TILES)))
                    n = item_of(half, 0) + 1 + k
                    round_item(n, x_hi[:, k, :], raw[:, n % 2, :])

            def keys(half, pair=None, per_tile=()):
                if half == 0:
                    begin_half(0)
                    round_tile(16 * (item_of(0, 1) // 2 + 1), 1)
                if half == 0:
                    for j in range(2):
                        round_item(item_of(0, 1) + 1 + j, wn_hi[:, 4 * j:4 * j + 4, :].rearrange("p k n -> p (k n)"),
                                   raw[:, j, 0:4 * VN])
                tiles(half, 0, KEY_TILES, False, pair, per_tile)
                act.wait_ge(stored[0], 16 * (half * N_TILES // 2 + 2))
                if half == 1:
                    act.wait_ge(ki_lo_ok, 1)
                for r in range(2):
                    act.dma_start(ki_raw[HD * r:HD * r + HD, :],
                                  proj[ROW_KI:ROW_KI + HD, half * HALF:(half + 1) * HALF]).then_inc(ki_in, 16)
                for j in range(NPAIR):
                    b = half * NPAIR + j
                    act.wait_ge(norm_mm, b + 1)
                    bank = 2 * (j % 2)
                    copy(vw[:, b, 0:HD], psum[:, bank, 0:HD])
                    copy(vw[:, b, HD + 1:VN + 1], psum[:, bank, HD:VN]).then_inc(norm_out, 1)
                act.wait_ge(ki_in, 32 * (half + 1))
                copy(ki_hi[:, half * HALF:(half + 1) * HALF], ki_raw[:, :]).then_inc(ki_hi_ok, 1)

            def queries(p):
                act.wait_ge(qi_in, 32 * p)
                if p > 1:
                    act.wait_ge(dots, 2 * chunks_before(p))
                copy(qi_split[:, :, :], qi_raw[:, :, :]).then_inc(qi_hi_ok, 1)

            def index_relu(p, j, c, w, bank0):
                n_dots = 2 * (chunks_before(p) + j * len(chunks(p)) + c // 512)
                for h in (0, 2):
                    act.wait_ge(dots, n_dots + 1)
                    if n_dots >= 2:
                        act.wait_ge(summed, 2 * (n_dots - 1))
                    nc.scalar.activation(relu[:, h:h + 2, 0:w], psum[:, bank0 + h:bank0 + h + 2, 0:w], ACT.Relu,
                                         scale=IH ** -0.5 * HD ** -0.5).then_inc(relued, 1)
                    n_dots += 1

            def whole_index(p):
                if p > 1:
                    store_masks(p - 1)
                for j in range(2):
                    for c, w in chunks(p):
                        index_relu(p, j, c, w, 4)

            for kind, *what in PLAN:
                {"keys": keys, "queries": queries, "index": whole_index, "tiles": tiles}[kind](*what)

            for i, stage in enumerate((qa_raw, qb_raw)):
                ks = slice(HALF * i, HALF * (i + 1))
                act.wait_ge(stage_in[i], 32)
                copy(ka_ext[0:HD, 0, ks], flat(stage[0:HD, :, :])).then_inc(setup_dve, 1)
                copy(ka_ext[0:HD, 1, ks], flat(stage[0:HD, :, :]))
                copy(ka_mix[HD:P, ks], flat(stage[HD:P, :, :])).then_inc(keys_taken, 1)
            act.wait_ge(stage_in[2], 32)
            copy(sel[:, 0:4, :], gate_a[0:H, :, :])
            copy(sel[:, 4:8, :], gate_b[0:H, :, :])
            for i in range(4):
                copy(ident4[:, i, :], ident[:, :])
            act.wait_ge(sink_in, 16)
            copy(sink8[:, :], sink1[:, :], scale=8.0).then_inc(setup_act, 1)

            def round_qb(b):
                j0 = HD if b == 0 else 0
                act.wait_ge(qb_in, 64 * (b + 1))
                if b:
                    act.wait_ge(b_logits, b)
                copy(qb_mix[:, :, :], qb_raw[:, :, :])
                copy(kb_hi[:, :, j0:WIN], kb_raw[:, :, j0:WIN]).then_inc(qb_round, 1)

            def round_qa(b):
                s = b % 2
                act.wait_ge(qa_in, 32 * (b + 1))
                if b >= 2:
                    act.wait_ge(a_used, units_to(b - 2))
                copy(qa_ext[0:HD, s, :, :], qa_raw[0:HD, :, :])
                copy(qa_mix[:, s, :, :], qa_raw[:, :, :]).then_inc(qa_round, 1)

            round_qb(0)
            round_qa(0)
            def exp_b(b, h):
                j0 = HD if b == 0 else 0
                if h == 0:
                    act.wait_ge(b_max, b + 1)
                    nc.scalar.activation(ez[:, :], zb[:, :], ACT.Exp)
                last = nc.scalar.activation(lb[:, h, j0:WIN], lb[:, h, j0:WIN], ACT.Exp, bias=nmb[:, h:h + 1],
                                            scale=0.125, accum_out=sum_b[:, h:h + 1])
                if h == H - 1:
                    last.then_inc(b_exp, 1)

            def turn_b(b):
                act.wait_ge(b_turned, b + 1)
                if b:
                    act.wait_ge(b_mixed, b)
                    copy(flat(ptb_prev[HD:P, :, :]), psum[0:HD, 2:4, :].rearrange("p b n -> p (b n)"))
                copy(flat(ptb_own[:, :, :]), psum[:, 0:2, :].rearrange("p b n -> p (b n)")).then_inc(b_pt, 1)

            def exp_a(b, kt, g):
                unit = units_to(b - 1) + 2 * kt + g
                act.wait_ge(a_logits, unit + 1)
                if unit >= 3:
                    act.wait_ge(a_used, unit - 2)
                nc.scalar.activation(prob[:, unit % 3, :], psum[:, 4 + unit % 2, :], ACT.Exp,
                                     scale=0.125).then_inc(a_prob, 1)

            def leave_a(b):
                act.wait_ge(a_used, units_to(b))
                if b:
                    act.wait_ge(a_turned, b)
                copy(out_a[:, :, :], psum[0:65, 6:8, :]).then_inc(a_outsb, 1)

            def round_y(b):
                s = b % 2
                act.wait_ge(y_in[s], 16 * (b // 2 + 1))
                if b >= 2:
                    act.wait_ge(o_mm, b - 1)
                copy(yt_hi[:, s, :, :], yt_raw[:, s, :, :]).then_inc(yt_hi_ok, 1)

            def round_w_out(k):
                act.wait_ge(wo_in[k % 2], 16 * (k // 2 + 1))
                copy(wo_hi[:, k, :], wo_raw[:, k % 2, :]).then_inc(wo_hi_ok, 1)

            run_steps({"queries": queries, "dots": lambda p, j, c, w: index_relu(p, j, c, w, 0), "exp_b": exp_b,
                       "turn_b": turn_b, "next_b": round_qb, "unit": exp_a, "leave_a": leave_a,
                       "next_a": round_qa, "w_out": round_w_out, "split_y": round_y, "count": count_step})

            def store_rows(b):
                act.wait_ge(o_done, b + 1)
                act.dma_start(out[P * b:P * b + P, :], z[:, b % 3, :]).then_inc(out_dma[b % 3], 16)

            for b in range(2, NB):
                round_y(b)
                store_rows(b - 2)
            store_rows(NB - 2)
            store_rows(NB - 1)

        @block.tensor
        def _(pe):
            def tile_products(g, n, u, x_items=None, x_last=False):
                pe.wait_ge(lo_done, n + 1)
                wait_if(pe, tile_out, g - 1)
                for k in range(KT):
                    if x_items is not None:
                        pe.wait_ge(lo_done, x_items + k + 1)
                    for m in range(2):
                        for q, (wt, xt) in enumerate(((w_hi, x_hi), (w_hi, x_lo), (w_lo, x_hi))):
                            last = pe.matmul(psum[:, 2 * u + m, :], wt[:, u, k, :], xt[:, k, 512 * m:512 * m + 512],
                                             start=(k == 0 and q == 0), stop=(k == KT - 1 and q == 2))
                    if x_last and k < KT - 1:
                        last.then_inc(x_used, 1)
                last.then_inc(tile_mm, 1)

            def tiles(half, first, n):
                g0 = half * N_TILES + first
                base = item_of(half, first)
                if first == 0:
                    for u in range(2):
                        tile_products(g0 + u, item_of(half, u), u, item_of(half, 0) + 1 if u == 0 else None)
                    g0, base, n = g0 + 2, item_of(half, 2), n - 2
                ends_x = half == 0 and first + n == N_TILES
                if ends_x:
                    n -= 2

                def body(i):
                    for u in range(2):
                        tile_products(i * 2 + (g0 + u), i * 2 + (base + u), u)

                tile_pairs(pe, g0, n, body)
                if ends_x:
                    for u in range(2):
                        tile_products(N_TILES - 2 + u, item_of(0, N_TILES - 2 + u), u, None, x_last=(u == 1))

            def keys(half):
                tiles(half, 0, KEY_TILES)
                pe.wait_ge(tile_out, half * N_TILES + KEY_TILES)
                for j in range(NPAIR):
                    b = half * NPAIR + j
                    if j >= 2:
                        pe.wait_ge(norm_out, b - 1)
                    toks = slice(P * j, P * j + P)
                    for k in range(KT):
                        for q, (xt, wt) in enumerate(((x_hi, wn_hi), (x_hi, wn_lo), (x_lo, wn_hi))):
                            last = pe.matmul(psum[:, 2 * (j % 2), 0:VN], xt[:, k, toks], wt[:, k, :],
                                             start=(k == 0 and q == 0), stop=(k == KT - 1 and q == 2))
                    last.then_inc(norm_mm, 1)
                pe.wait_ge(norm_out, NPAIR * (half + 1))
                pe.wait_ge(ki_lo_ok, half + 1)

            def index_dots(p, j, c, w, bank0):
                n_dots = 2 * (chunks_before(p) + j * len(chunks(p)) + c // 512)
                for h0 in (0, 2):
                    if n_dots >= 2:
                        pe.wait_ge(relued, n_dots - 1)
                    for h in range(h0, h0 + 2):
                        pe.matmul(psum[:, bank0 + h, 0:w], qi_split[:, h, P * j:P * j + P],
                                  ki_hi[:, c:c + w], start=True, stop=False)
                        last = pe.matmul(psum[:, bank0 + h, 0:w], qi_split[0:HD, h, P * j:P * j + P],
                                         ki_lo[:, c:c + w], start=False, stop=True)
                    last.then_inc(dots, 1)
                    n_dots += 1

            def whole_index(p):
                pe.wait_ge(qi_lo_ok, p)
                for j in range(2):
                    for c, w in chunks(p):
                        index_dots(p, j, c, w, 4)

            for kind, *what in PLAN:
                if kind == "keys":
                    keys(what[0])
                elif kind == "index":
                    whole_index(what[0])
                elif kind == "tiles":
                    tiles(*what[:3])

            pe.wait_ge(tile_out, 2 * N_TILES)
            pe.wait_ge(setup_act, 1)
            pe.wait_ge(late_in, 16 * 6)
            pe.wait_ge(setup_pool, 3)

            def window_logits(b):
                j0 = HD if b == 0 else 0
                pe.wait_ge(qb_split, b + 1)
                if b - 1 in INDEX_AT:
                    pe.wait_ge(relued, 2 * chunks_before(INDEX_AT[b - 1] + 1))
                if b >= 2:
                    pe.wait_ge(a_gated, b - 1)
                if b:
                    pe.wait_ge(b_gated, b)
                for h in range(H):
                    o = psum[:, h // 2, WIN * (h % 2) + j0:WIN * (h % 2) + WIN]
                    pe.matmul(o, qb_mix[:, h, :], kb_hi[:, h // 4, j0:WIN], start=True, stop=False)
                    last = pe.matmul(o, qb_mix[0:HD, h, :], kb_lo[:, h // 4, j0:WIN], start=False, stop=True)
                last.then_inc(b_logits, 1)

            def max_logits(b, h, c):
                s = b % 2
                n_keys = P * (b + 1)
                if (h, c) == (0, 0):
                    pe.wait_ge(qa_round, b + 1)
                    pe.wait_ge(qa_zero, b + 1)
                    pe.wait_ge(b_biased, b + 1)
                    if b:
                        pe.wait_ge(pos_ok, b)
                scan = scans_to(b - 1) + h * (1 + (b >= 8)) + c // 1024
                if scan >= 2:
                    pe.wait_ge(a_scanned, scan - 1)
                for k0 in range(c, min(c + 1024, n_keys), 512):
                    w = min(512, n_keys - k0)
                    bank = 2 * (scan % 2) + (k0 - c) // 512
                    diag = k0 + w == n_keys
                    last = pe.matmul(psum[:, bank, 0:w], qa_ext[:, s, h, :], ka_ext[:, s, k0:k0 + w],
                                     start=True, stop=not diag)
                    if diag:
                        last = pe.matmul(psum[:, bank, w - P:w], power[:, h, :], upper[:, 0, :],
                                         start=False, stop=True)
                last.then_inc(a_scan, 1)

            def turn_b(b):
                pe.wait_ge(b_exp, b + 1)
                pe.wait_ge(a_scanned, scans_to(b))
                for h in range(H):
                    last = pe.transpose(psum[:, h // 4, P * (h % 4):P * (h % 4) + P], lb[:, h, HD:WIN],
                                        ident[:, :])
                    if b:
                        last = pe.transpose(psum[0:HD, 2 + h // 4, P * (h % 4):P * (h % 4) + P],
                                            lb[:, h, 0:HD], ident[:, :])
                last.then_inc(b_turned, 1)

            def minus_max(b):
                pe.wait_ge(a_neg, b + 1)
                pe.wait_ge(b_pt, b + 1)
                pe.transpose(psum[0:H, 1, 0:P], neg_max[:, :], ident[:, :]).then_inc(a_negt, 1)

            def mix_b(b):
                for h in range(H):
                    o = psum[:, 0, HD * h:HD * h + HD]
                    v0 = HD + 1 + HD * (h // 4)
                    if b:
                        pe.matmul(o, ptb_prev[HD:P, h, :], vw[HD:P, b - 1, v0:v0 + HD], start=True, stop=False)
                    last = pe.matmul(o, ptb_own[:, h, :], vw[:, b, v0:v0 + HD], start=(b == 0), stop=True)
                last.then_inc(b_mixed, 1)

            def unit_logits(b, kt, g):
                s = b % 2
                u = units_to(b - 1) + 2 * kt + g
                if u >= 2:
                    pe.wait_ge(a_prob, u - 1)
                o = psum[:, 4 + u % 2, :]
                ks = slice(P * kt, P * kt + P)
                hs = slice(4 * g, 4 * g + 4)
                pe.matmul(o, mask[:, s, ks], flat(ident4[:, :, :]), start=True, stop=False)
                pe.matmul(o, ka_mix[:, ks], flat(qa_mix[:, s, hs, :]), start=False, stop=False)
                last = pe.matmul(o, ka_ext[:, s, ks], flat(qa_ext[:, s, hs, :]), start=False, stop=(kt < b))
                if kt == b:
                    pe.matmul(o, upper[:, 0, :], flat(power[:, hs, :]), start=False, stop=False)
                    last = pe.matmul(o, upper[:, 1, :], flat(power[:, hs, :]), start=False, stop=True)
                last.then_inc(a_logits, 1)

            def unit(b, kt, g):
                u = units_to(b - 1) + 2 * kt + g
                if (kt, g) == (0, 0):
                    if b >= 2:
                        pe.wait_ge(mask_in[b % 2], 16 * (b // 2))
                    else:
                        pe.wait_ge(setup_dve, 3)
                    pe.wait_ge(qa_split, b + 1)
                    pe.wait_ge(a_ext, b + 1)
                    unit_logits(b, 0, 0)
                    if b:
                        pe.wait_ge(a_outsb, b)
                if (kt, g) != (b, 1):
                    unit_logits(b, kt + g, 1 - g)
                pe.wait_ge(a_prob, u + 1)
                pe.matmul(psum[0:65, 6 + g, :], vw[:, kt, 0:65], prob[:, u % 3, :],
                          start=(kt == 0), stop=(kt == b)).then_inc(a_used, 1)

            def turn_a(b):
                pe.wait_ge(a_outsb, b + 1)
                pe.wait_ge(b_pt, min(b + 2, NB))
                if b + 1 in INDEX_AT:
                    pe.wait_ge(relued, 2 * chunks_before(INDEX_AT[b + 1] + 1))
                for h in range(H):
                    last = pe.transpose(psum[:, 2 + h // 4, 65 * (h % 4):65 * (h % 4) + 65],
                                        out_a[:, h // 4, P * (h % 4):P * (h % 4) + P], ident[0:65, 0:65])
                last.then_inc(a_turned, 1)

            def columns(y, bank, done):
                for t in range(4):
                    last = pe.transpose(psum[:, bank, P * t:P * t + P],
                                        y[:, 2 * t:2 * t + 2, :].rearrange("p h d -> p (h d)"), ident[:, :])
                last.then_inc(done, 1)

            def columns_a(b):
                pe.wait_ge(a_y, b + 1)
                columns(y_a, 1, a_yt)

            def columns_b(b):
                pe.wait_ge(b_y, b + 1)
                columns(y_b, 0, b_yt)

            def index(p):
                b = {pair: at for at, pair in INDEX_AT.items()}[p]
                pe.wait_ge(b_gated, b + 1)
                pe.wait_ge(qi_lo_ok, p)

            def project(b):
                s = b % 2
                if b == 0:
                    pe.wait_ge(wo_lo_ok, KT)
                    pe.wait_ge(a_used, units_to(NB - 1))
                if b == 1:
                    pe.wait_ge(a_outsb, NB)
                pe.wait_ge(yt_lo_ok, b + 1)
                if b >= 2:
                    pe.wait_ge(o_z, b - 1)
                for m in range(2):
                    cols = slice(512 * m, 512 * m + 512)
                    for k in range(KT):
                        for q, (yt, wt) in enumerate(((yt_hi, wo_hi), (yt_hi, wo_lo), (yt_lo, wo_hi))):
                            last = pe.matmul(psum[:, 4 + 2 * s + m, :], yt[:, s, k, :], wt[:, k, cols],
                                             start=(k == 0 and q == 0), stop=(k == KT - 1 and q == 2))
                last.then_inc(o_mm, 1)

            run_steps({"index": index, "dots": lambda p, j, c, w: index_dots(p, j, c, w, 0), "turn_a": turn_a,
                       "columns_a": columns_a, "window": window_logits, "max_logits": max_logits, "turn_b": turn_b,
                       "minus_max": minus_max, "mix_b": mix_b, "columns_b": columns_b, "unit": unit,
                       "project": project})

            for b in range(1, NB):
                project(b)

        @block.vector
        def _(dve):
            v = nc.vector
            done = {"prep": 0, "trial": 0, "count": 0, "sum": 0, "b_step": 0}

            def step(ins):
                ins.then_inc(prep, 1)
                done["prep"] += 1
                dve.wait_ge(prep, done["prep"])

            def small(ins):
                ins.then_inc(b_step, 1)
                done["b_step"] += 1
                dve.wait_ge(b_step, done["b_step"])

            def index_begin(p):
                if p > 1:
                    dve.wait_ge(mask_out, 32 * (p - 1))

            def index_sum(p, j, c, w):
                n_chunk = chunks_before(p) + j * len(chunks(p)) + c // 512
                b = 2 * p + j
                dve.wait_ge(norm_out, b + 1)
                o = score[:, j, c:c + w]
                for h in range(IH):
                    if h % 2 == 0:
                        dve.wait_ge(relued, 2 * n_chunk + h // 2 + 1)
                    wt = vw[:, b, VN + 1 - IH + h:VN + 2 - IH + h]
                    if h == 0:
                        v.tensor_scalar(o, relu[:, h, 0:w], wt, 0.0, ALU.mult, ALU.add).then_inc(summed, 1)
                    else:
                        dve.wait_ge(summed, done["sum"])
                        v.scalar_tensor_tensor(o, relu[:, h, 0:w], wt, o, ALU.mult, ALU.add).then_inc(summed, 1)
                    done["sum"] += 1

            def sortable(p):
                n = nd(p)
                dve.wait_ge(summed, done["sum"])
                low = -3.0e38
                v.memset(score[0:HD, 0, n - P - HD:n - P], low)
                v.memset(score[0:HD, 1, n - HD:n], low)
                step(v.memset(score[:, 0, n - P:n], low))
                sc = score[:, :, 0:n].bitcast(I32)
                di = dist[:, :, 0:n].bitcast(I32)
                step(v.tensor_scalar(di, sc, 31, 0x7fffffff, ALU.arith_shift_right, ALU.bitwise_and))
                step(v.tensor_tensor(sc, sc, di, ALU.bitwise_xor))
                step(v.tensor_scalar(di, sc, -65536, None, ALU.bitwise_and))

            def count_step(p, i):
                n = nd(p)
                part = i // 16
                u = trial[:, part, :]
                if i == 0:
                    v.memset(u, -32768.0).then_inc(trial_ok, 1)
                    done["trial"] += 1
                if i == 16:
                    dve.wait_ge(trial_ok, done["trial"])
                    for j in range(2):
                        lows = score[:, j, 0:n].bitcast(U16).rearrange("p (n t) -> p n t", t=2)[:, :, 0]
                        last = v.scalar_tensor_tensor(dist[:, j, 0:n], dist[:, j, 0:n].bitcast(I32),
                                                      trial[:, 0, j:j + 1], lows, ALU.subtract, ALU.add)
                    step(last)
                    v.memset(u, 32767.5).then_inc(trial_ok, 1)
                    done["trial"] += 1
                dve.wait_ge(trial_ok, done["trial"])
                src = dist[:, 0, 0:n].bitcast(I32) if part == 0 else dist[:, 0, 0:n]
                v.tensor_scalar(above[:, 0, 0:n], src, u[:, 0:1], None, ALU.is_ge, ALU.add,
                                accum_out=count[:, 0:1]).then_inc(counted, 1)
                done["count"] += 1

            def decide(p, i):
                n = nd(p)
                u = trial[:, i // 16, :]
                dve.wait_ge(counted, done["count"])
                v.tensor_scalar(accept[:, 0:1], count[:, 0:1], float(TOPK), 0.5, ALU.is_ge, ALU.subtract)
                dve.wait_ge(signed, done["count"])
                v.tensor_scalar(accept[:, 1:2], count[:, 1:2], float(n - 2 * TOPK), 0.5, ALU.is_le,
                                ALU.subtract).then_inc(accepted, 1)
                dve.wait_ge(accepted, done["count"])
                v.scalar_tensor_tensor(u, accept[:, :], steps[:, i:i + 1], u, ALU.mult, ALU.add) \
                    .then_inc(trial_ok, 1)
                done["trial"] += 1

            def make_masks(p):
                n = nd(p)
                dve.wait_ge(trial_ok, done["trial"])
                for j in range(2):
                    t = trial[:, 1, j:j + 1]
                    v.tensor_scalar(above[:, j, 0:n], dist[:, j, 0:n], t, None, ALU.is_gt, ALU.add,
                                    accum_out=n_above[:, j:j + 1])
                    last = v.tensor_scalar(equal[:, j, 0:n], dist[:, j, 0:n], t, None, ALU.is_equal)
                step(last)
                for j in range(2):
                    last = v.tensor_tensor_scan(rank[:, j, 0:n], equal[:, j, 0:n], equal[:, j, 0:n],
                                                n_above[:, j:j + 1], ALU.add, ALU.max)
                step(last)
                step(v.scalar_tensor_tensor(equal[:, :, 0:n], rank[:, :, 0:n], float(TOPK), equal[:, :, 0:n],
                                            ALU.is_le, ALU.mult))
                step(v.scalar_tensor_tensor(above[:, :, 0:n], equal[:, :, 0:n], -1.0, above[:, :, 0:n],
                                            ALU.add, ALU.add))
                v.tensor_scalar(above[:, :, 0:n], above[:, :, 0:n], BIG, None, ALU.mult).then_inc(mask_ok, 1)

            dve.wait_ge(const_in, 32)
            def search_tiles(pair=None, per_tile=()):
                for _ in range(sum(per_tile)):
                    i = done["count"] % 32
                    count_step(pair, i)
                    decide(pair, i)
                    if i == 31:
                        make_masks(pair)

            for kind, *what in PLAN:
                if kind == "index":
                    p = what[0]
                    index_begin(p)
                    for j in range(2):
                        for c, w in chunks(p):
                            index_sum(p, j, c, w)
                    sortable(p)
                elif kind == "keys":
                    search_tiles(*what[1:])
                elif kind == "tiles":
                    search_tiles(*what[4:])

            for i in range(2):
                dve.wait_ge(stored[i], 16 * N_TILES)
            dve.wait_ge(late_in, 16 * 6)
            dve.wait_ge(setup_act, 1)
            v.memset(mask[:, 0, 0:P], 0.0)
            step(v.memset(mask[:, 1, 0:2 * P], 0.0))
            v.memset(mask[0:HD, 0, HD:P], -BIG)
            step(v.memset(mask[0:HD, 1, P + HD:2 * P], -BIG))
            v.tensor_scalar(ka_ext[96:98, 1, :], ka_ext[96:98, 1, :].bitcast(F32), -float(P), None,
                            ALU.add).then_inc(pos_ok, 1)
            v.memset(mb[:, :], 0.0).then_inc(setup_dve, 1)

            def window(b):
                j0 = HD if b == 0 else 0
                dve.wait_ge(b_logits, b + 1)
                if b:
                    dve.wait_ge(b_turned, b)
                ps = psum[:, 0:4, 0:2 * WIN].rearrange("p b (h j) -> p b h j", h=2)[:, :, :, j0:WIN]
                four = lambda t: t[:, :, :].rearrange("p (b h) j -> p b h j", h=2)[:, :, :, j0:WIN]
                if b == 0:
                    dve.wait_ge(bias_in, 16)
                v.tensor_tensor(four(lb), ps, four(bias), ALU.add).then_inc(b_biased, 1)
                dve.wait_ge(b_biased, b + 1)
                small(v.tensor_reduce(mb[:, :], lb[:, :, j0:WIN], AX_X, ALU.max))
                small(v.tensor_tensor(mb2[:, :], mb[:, :], sink8[:, :], ALU.max))
                small(v.tensor_scalar(nmb[:, :], mb2[:, :], -0.125, None, ALU.mult))
                v.tensor_tensor(zb[:, :], nmb[:, :], sink1[:, :], ALU.add).then_inc(b_max, 1)

            def scan_max(b, h, c):
                s = b % 2
                n_keys = P * (b + 1)
                if b >= 2 and (h, c) == (0, 0):
                    dve.wait_ge(mask_in[s], 16 * (b // 2))
                scan = scans_to(b - 1) + h * (1 + (b >= 8)) + c // 1024
                w = min(1024, n_keys - c)
                dve.wait_ge(a_scan, scan + 1)
                if scan >= 2:
                    dve.wait_ge(a_scanned, scan - 1)
                src = psum[:, 2 * (scan % 2):2 * (scan % 2) + 2, :].rearrange("p b n -> p (b n)")[:, 0:w]
                v.tensor_tensor_reduce(out=junk[:, scan % 2, 0:w], in0=src, in1=mask[:, s, c:c + w],
                                       scale=1.0, scalar=-3.0e38, op0=ALU.add, op1=ALU.max,
                                       accum_out=part_max[:, c // 1024, h:h + 1]).then_inc(a_scanned, 1)
                scan += 1
                if scan < scans_to(b):
                    return
                dve.wait_ge(a_scanned, scan)
                if n_keys > 1024:
                    small(v.tensor_tensor(neg_max[:, :], part_max[:, 0, :], part_max[:, 1, :], ALU.max))
                    v.tensor_scalar(neg_max[:, :], neg_max[:, :], -1.0, None, ALU.mult).then_inc(a_neg, 1)
                else:
                    v.tensor_scalar(neg_max[:, :], part_max[:, 0, :], -1.0, None, ALU.mult).then_inc(a_neg, 1)

            def minus_max(b):
                s = b % 2
                dve.wait_ge(b_exp, b + 1)
                small(v.tensor_tensor(den_b[:, :], sum_b[:, :], ez[:, :], ALU.add))
                small(v.reciprocal(rec_b[:, :], den_b[:, :]))
                dve.wait_ge(a_negt, b + 1)
                v.tensor_tensor(qa_ext[HD:HD + H, s, :, :], psum[0:H, 1, 0:P].unsqueeze(1).broadcast_to([H, H, P]),
                                sel[:, :, :], ALU.mult).then_inc(a_ext, 1)

            def mix_b(b):
                dve.wait_ge(b_mixed, b + 1)
                if b:
                    dve.wait_ge(b_yt, b)
                v.tensor_tensor(y_b[:, :, :], psum[:, 0, :].rearrange("p (h d) -> p h d", h=H),
                                rec_b[:, :].unsqueeze(2).broadcast_to([P, H, HD]), ALU.mult).then_inc(b_y, 1)

            def gate_group(b, turned, bank, y, gate, gate_in, was_stored, gated):
                dve.wait_ge(turned, b + 1)
                dve.wait_ge(gate_in, 16 * (b + 1))
                if b:
                    dve.wait_ge(was_stored, 16 * b)
                v.tensor_tensor(flat(y[:, :, :]), psum[:, bank, :], flat(gate[:, :, :]), ALU.mult) \
                    .then_inc(gated, 1)

            def turn_a(b):
                dve.wait_ge(a_turned, b + 1)
                heads = [psum[:, 2 + g, 0:4 * 65].rearrange("p (h d) -> p h d", h=4) for g in range(2)]
                for g in range(2):
                    last = v.reciprocal(rec_a[:, 4 * g:4 * g + 4], heads[g][:, :, HD])
                last.then_inc(a_rec, 1)
                dve.wait_ge(a_rec, b + 1)
                for g in range(2):
                    last = v.tensor_tensor(y_a[:, 4 * g:4 * g + 4, :], heads[g][:, :, 0:HD],
                                           rec_a[:, 4 * g:4 * g + 4].unsqueeze(2).broadcast_to([P, 4, HD]),
                                           ALU.mult)
                last.then_inc(a_y, 1)
                if b + 2 < NB:
                    s = b % 2
                    v.tensor_scalar(ka_ext[96:98, s, :], ka_ext[96:98, s, :].bitcast(F32), -2.0 * P, None,
                                    ALU.add).then_inc(pos_ok, 1)

            run_steps({
                "index": index_begin, "dots": index_sum, "sortable": sortable, "count": count_step,
                "decide": decide,
                "masks": make_masks, "turn_a": turn_a, "window": window, "scan": scan_max,
                "columns_a": lambda b: gate_group(b, a_yt, 1, yt_a, gate_a, gate_a_in, a_stored, a_gated),
                "minus_max": minus_max, "mix_b": mix_b,
                "columns_b": lambda b: gate_group(b, b_yt, 0, yt_b, gate_b, gate_b_in, b_stored, b_gated)})

            dve.wait_ge(ln_in, 32)
            n_o = 0
            for b in range(NB):
                s = b % 2
                r = z[:, b % 3, :]
                dve.wait_ge(o_mm, b + 1)
                dve.wait_ge(row_in[s], 16 * (b // 2 + 1))
                if b >= 3:
                    dve.wait_ge(out_dma[b % 3], 16 * (b // 3))
                v.scalar_tensor_tensor(r, x_row[:, s, :], ALPHA, psum[:, 4 + 2 * s:6 + 2 * s, :]
                                       .rearrange("p b n -> p (b n)"), ALU.mult, ALU.add).then_inc(o_z, 1)
                dve.wait_ge(o_z, b + 1)
                for m in range(2):
                    last = v.bn_stats(stats[:, m, :], r[:, 512 * m:512 * m + 512])
                last.then_inc(o_step, 1)
                dve.wait_ge(o_step, n_o + 1)
                v.bn_aggr(moments[:, s, :], stats[:, :, :]).then_inc(o_step, 1)
                dve.wait_ge(o_step, n_o + 2)
                v.tensor_scalar(var_eps[:, s:s + 1], moments[:, s, 1:2], EPS, None, ALU.add).then_inc(o_var, 1)
                dve.wait_ge(o_rstd, b + 1)
                v.tensor_scalar(r, r, moments[:, s, 0:1], rstd[:, s:s + 1], ALU.subtract, ALU.mult) \
                    .then_inc(o_step, 1)
                dve.wait_ge(o_step, n_o + 3)
                v.tensor_tensor(r, r, gains[:, :], ALU.mult).then_inc(o_step, 1)
                dve.wait_ge(o_step, n_o + 4)
                v.tensor_tensor(r, r, shifts[:, :], ALU.add).then_inc(o_done, 1)
                n_o += 4


def round12(a):
    bits = a.view(np.uint32)
    odd = (bits >> np.uint32(12)) & np.uint32(1)
    return ((bits + np.uint32(0x7FF) + odd) & np.uint32(0xFFFFF000)).view(np.float32)


def shape_constants():
    slopes = np.array([2.0 ** (-8.0 * (i + 1) / (2 * H)) for i in range(2 * H)], np.float32)
    sa, sbl = slopes[0::2] * np.float32(8), slopes[1::2] * np.float32(8)
    sa_hi = round12(sa)
    sa_lo = sa - sa_hi
    eye = np.eye(P, dtype=np.float32)
    q = np.arange(P)
    upper = np.maximum(q[None, :] - q[:, None], 0).astype(np.float32)
    power = np.stack([-2.0 * 8 * 2.0 ** -h * eye for h in range(H)], 1).astype(np.float32)
    upper = upper * slopes[0]
    upper_hi = round12(upper)
    upper = np.stack([upper_hi, upper - upper_hi], 1)
    extm = np.zeros((P - HD, H, P), np.float32)
    extm[32] = sa_hi[:, None]
    extm[33] = sa_lo[:, None]
    extk = np.zeros((P - HD, L), np.float32)
    extk[0:H] = 1.0
    extk[32:34] = np.arange(L)
    j = np.arange(WIN)
    dist = np.abs(q[:, None] + HD - j[None, :]).astype(np.float32)
    seen = np.where(q[:, None] < HD, j[None, :] < P, j[None, :] >= HD)
    bias = np.where(seen[:, None, :], -sbl[None, :, None] * dist[:, None, :], np.float32(-BIG)).astype(np.float32)
    sel = np.repeat(np.eye(H, dtype=np.float32)[:, :, None], P, 2)
    steps = np.repeat(np.array([2.0 ** (31 - i) for i in range(32)], np.float32)[None], P, 0)
    return dict(c_step=steps, c_ident=eye, c_upper=upper, c_pow=power, c_extm=extm,
                c_extk=extk, c_bias=bias, c_sel=sel)

def kernel(**inputs):
    import concourse.bacc as bacc
    from concourse.bass_utils import run_bass_kernel_spmd

    nc = bacc.Bacc("TRN2", target_bir_lowering=False, num_devices=1)
    x = np.ascontiguousarray(inputs["x"])[0]
    w = np.ascontiguousarray(inputs["w_in"])[0]
    order = np.r_[1152:1408, 1408:1472, 512:576, 1988:2116, 0:512, 1476:1988, 640:1152, 2244:2756]
    w_tiles = w[:, order].reshape(KT, P, N_TILES, P).transpose(2, 1, 0, 3).reshape(N_TILES, P, KT * P)
    w_norm = w[:, np.r_[576:640, 2116:2244, 1472:1476]].reshape(KT, P, VN).transpose(1, 0, 2)
    w_out = np.asarray(inputs["w_out"])[0].reshape(KT, P, D).transpose(1, 0, 2)
    arrays = dict(xT=x.T, w_tiles=w_tiles, w_norm=w_norm, w_out=w_out, x_res=x,
                  sinks=np.asarray(inputs["sinks"]), ln_g=np.asarray(inputs["ln_g"]),
                  ln_b=np.asarray(inputs["ln_b"]), **shape_constants())
    arrays = {k: np.ascontiguousarray(a) for k, a in arrays.items()}
    args = {k: nc.dram_tensor(k, a.shape, F32, kind="ExternalInput").ap() for k, a in arrays.items()}
    args["proj"] = nc.dram_tensor("proj", (N_TILES * P, L), F32, kind="Internal").ap()
    args["masks"] = nc.dram_tensor("masks", (NB, P, L), BF16, kind="Internal").ap()
    args["y_t"] = nc.dram_tensor("y_t", (D, L), F32, kind="Internal").ap()
    args["out"] = nc.dram_tensor("out", (1, L, D), F32, kind="ExternalOutput").ap().rearrange("a l d -> (a l) d")
    hybrid_kernel(nc, **args)
    r = run_bass_kernel_spmd(nc, [arrays], core_ids=[0])
    return r.results[0]["out"]
```
